# Optimizing a Trainium2 kernel written in Bass

```python
import math
import jax, jax.numpy as jnp
from jax import lax
import numpy as np

D_MODEL = 1024
BATCH = 1
SEQ = 256
DEPTH = 1

CHUNK = 64
RNN_WIDTH = 1024
RNN_BLOCKS = 16
RNN_BLOCK_DIM = RNN_WIDTH // RNN_BLOCKS
CONV_WIDTH = 4
LRU_C = 8.0
FOX_HEADS = 16
FOX_HEAD_DIM = 64
FOX_WIDTH = FOX_HEADS * FOX_HEAD_DIM
QUERY_BLOCK = 128
N_BRANCHES = 2
IN_COLS = 2 * RNN_WIDTH + 3 * FOX_WIDTH + FOX_HEADS + N_BRANCHES * D_MODEL
N_EXPERTS = 32
TOP_K = 4
D_FF = 1024
SWIGLU_LIMIT = 7.0
SWIGLU_ALPHA = 1.702
RMS_EPS = 1e-6

kernel_name = "hybrid_rglru_fox_moe_block"

def rmsnorm(x, g):
    xf = x.astype(jnp.float32)
    y = xf * lax.rsqrt(jnp.mean(xf * xf, axis=-1, keepdims=True) + RMS_EPS)
    return (y * g.astype(jnp.float32)).astype(x.dtype)

def causal_depthwise_conv(x, w, b):
    c = x.shape[-1]
    y = lax.conv_general_dilated(
        x, w[:, None, :].astype(x.dtype), window_strides=(1,),
        padding=[(CONV_WIDTH - 1, 0)],
        dimension_numbers=("NWC", "WIO", "NWC"), feature_group_count=c)
    return y + b.astype(x.dtype)

def _lin_combine(left, right):
    a_l, b_l = left
    a_r, b_r = right
    return a_l * a_r, a_r * b_l + b_r

def rg_lru(xc, w_rg, b_rg, w_ig, b_ig, lru_lambda):
    bsz, s, r = xc.shape
    xb = xc.reshape(bsz, s, RNN_BLOCKS, RNN_BLOCK_DIM)
    gate_r = jnp.einsum('bshi,hij->bshj', xb, w_rg).reshape(bsz, s, r) + b_rg
    gate_i = jnp.einsum('bshi,hij->bshj', xb, w_ig).reshape(bsz, s, r) + b_ig
    rt = jax.nn.sigmoid(gate_r.astype(jnp.float32))
    it = jax.nn.sigmoid(gate_i.astype(jnp.float32))
    log_a = -LRU_C * rt * jax.nn.softplus(-lru_lambda.astype(jnp.float32))
    a = jnp.exp(log_a)
    mult = jnp.sqrt(-jnp.expm1(2.0 * log_a))
    bterm = mult * (it * xc.astype(jnp.float32))
    nc = s // CHUNK
    a_c = a.reshape(bsz, nc, CHUNK, r).transpose(1, 0, 2, 3)
    b_c = bterm.reshape(bsz, nc, CHUNK, r).transpose(1, 0, 2, 3)

    def step(h0, ab):
        ac, bc = ab
        acum, bcum = lax.associative_scan(_lin_combine, (ac, bc), axis=1)
        h = acum * h0[:, None, :] + bcum
        return h[:, -1, :], h

    h0 = jnp.zeros((bsz, r), jnp.float32)
    _, hs = lax.scan(step, h0, (a_c, b_c))
    return hs.transpose(1, 0, 2, 3).reshape(bsz, s, r)

def forgetting_attention(q, k, v, cum_logf):
    s = q.shape[2]
    scale = 1.0 / math.sqrt(FOX_HEAD_DIM)
    outs = []
    for i in range(s // QUERY_BLOCK):
        q0 = i * QUERY_BLOCK
        q1 = q0 + QUERY_BLOCK
        logits = jnp.einsum('bhqd,bhkd->bhqk', q[:, :, q0:q1].astype(jnp.float32),
                            k[:, :, :q1].astype(jnp.float32)) * scale
        logits = logits + (cum_logf[:, :, q0:q1, None] - cum_logf[:, :, None, :q1])
        qpos = jnp.arange(q0, q1)[:, None]
        kpos = jnp.arange(q1)[None, :]
        logits = jnp.where(kpos <= qpos, logits, -jnp.inf)
        p = jax.nn.softmax(logits, axis=-1).astype(v.dtype)
        outs.append(jnp.einsum('bhqk,bhkd->bhqd', p, v[:, :, :q1]))
    return jnp.concatenate(outs, axis=2)

def moe_ffn(h, w_router, b_router, w_gate_up, b_gate_up, w_down, b_down):
    bsz, s, d = h.shape
    t = h.reshape(bsz * s, d)
    logits = (t @ w_router).astype(jnp.float32) + b_router.astype(jnp.float32)
    top_v, top_i = lax.top_k(logits, TOP_K)
    top_w = jax.nn.softmax(top_v, axis=-1)
    combine = jnp.sum(jax.nn.one_hot(top_i, N_EXPERTS, dtype=jnp.float32) * top_w[..., None], axis=1)
    combine = combine.astype(h.dtype)
    out = jnp.zeros_like(t)
    for e in range(N_EXPERTS):
        gu = t @ w_gate_up[e] + b_gate_up[e]
        gate = jnp.minimum(gu[:, :D_FF], SWIGLU_LIMIT)
        up = jnp.clip(gu[:, D_FF:], -SWIGLU_LIMIT, SWIGLU_LIMIT)
        glu = gate * jax.nn.sigmoid(SWIGLU_ALPHA * gate)
        y = ((up + 1.0) * glu) @ w_down[e] + b_down[e]
        out = out + combine[:, e:e + 1] * y
    return out.reshape(bsz, s, d)

def setup_inputs(seed: int = 0) -> dict:
    key = jax.random.key(seed)
    ks = jax.random.split(key, 24)
    f32 = jnp.float32
    nrm = lambda k, shape, scale: jax.random.normal(k, shape, f32) * scale
    u = jax.random.uniform(ks[9], (RNN_WIDTH,), f32, 0.9, 0.999)
    sig_l = u ** (1.0 / LRU_C)
    lru_lambda = jnp.log(sig_l) - jnp.log1p(-sig_l)
    return {
        "x": nrm(ks[0], (BATCH, SEQ, D_MODEL), 1.0),
        "g_mix": 1.0 + nrm(ks[1], (D_MODEL,), 0.02),
        "w_in": nrm(ks[2], (D_MODEL, IN_COLS), D_MODEL ** -0.5),
        "conv_w": nrm(ks[3], (CONV_WIDTH, RNN_WIDTH), CONV_WIDTH ** -0.5),
        "conv_b": nrm(ks[4], (RNN_WIDTH,), 0.01),
        "w_rg": nrm(ks[5], (RNN_BLOCKS, RNN_BLOCK_DIM, RNN_BLOCK_DIM), RNN_BLOCK_DIM ** -0.5),
        "b_rg": nrm(ks[6], (RNN_WIDTH,), 0.01),
        "w_ig": nrm(ks[7], (RNN_BLOCKS, RNN_BLOCK_DIM, RNN_BLOCK_DIM), RNN_BLOCK_DIM ** -0.5),
        "b_ig": nrm(ks[8], (RNN_WIDTH,), 0.01),
        "lru_lambda": lru_lambda,
        "b_f": 2.0 + nrm(ks[10], (FOX_HEADS,), 0.1),
        "w_lru_out": nrm(ks[11], (RNN_WIDTH, D_MODEL), RNN_WIDTH ** -0.5),
        "w_fox_out": nrm(ks[12], (FOX_WIDTH, D_MODEL), FOX_WIDTH ** -0.5),
        "w_o": nrm(ks[13], (D_MODEL, D_MODEL), D_MODEL ** -0.5),
        "g_ffn": 1.0 + nrm(ks[14], (D_MODEL,), 0.02),
        "w_router": nrm(ks[15], (D_MODEL, N_EXPERTS), D_MODEL ** -0.5),
        "b_router": nrm(ks[16], (N_EXPERTS,), 0.01),
        "w_gate_up": nrm(ks[17], (N_EXPERTS, D_MODEL, 2 * D_FF), D_MODEL ** -0.5),
        "b_gate_up": nrm(ks[18], (N_EXPERTS, 2 * D_FF), 0.01),
        "w_down": nrm(ks[19], (N_EXPERTS, D_FF, D_MODEL), D_FF ** -0.5),
        "b_down": nrm(ks[20], (N_EXPERTS, D_MODEL), 0.01),
        "g_final": 1.0 + nrm(ks[21], (D_MODEL,), 0.02),
    }

def reference(x, g_mix, w_in, conv_w, conv_b, w_rg, b_rg, w_ig, b_ig, lru_lambda, b_f,
              w_lru_out, w_fox_out, w_o, g_ffn, w_router, b_router, w_gate_up, b_gate_up,
              w_down, b_down, g_final):
    bsz, s, _ = x.shape
    for _layer in range(DEPTH):
        h = rmsnorm(x, g_mix)
        proj = h @ w_in
        o = 0
        lru_x = proj[..., o:o + RNN_WIDTH]; o += RNN_WIDTH
        lru_gate = proj[..., o:o + RNN_WIDTH]; o += RNN_WIDTH
        q = proj[..., o:o + FOX_WIDTH]; o += FOX_WIDTH
        k = proj[..., o:o + FOX_WIDTH]; o += FOX_WIDTH
        v = proj[..., o:o + FOX_WIDTH]; o += FOX_WIDTH
        f_logit = proj[..., o:o + FOX_HEADS]; o += FOX_HEADS
        gate_lru = proj[..., o:o + D_MODEL]; o += D_MODEL
        gate_fox = proj[..., o:o + D_MODEL]

        xc = causal_depthwise_conv(lru_x, conv_w, conv_b)
        hr = rg_lru(xc, w_rg, b_rg, w_ig, b_ig, lru_lambda)
        y_lru = (hr * jax.nn.gelu(lru_gate.astype(jnp.float32), approximate=True)).astype(x.dtype)

        to_heads = lambda z: z.reshape(bsz, s, FOX_HEADS, FOX_HEAD_DIM).transpose(0, 2, 1, 3)
        logf = jax.nn.log_sigmoid(f_logit.astype(jnp.float32) + b_f.astype(jnp.float32))
        cum_logf = jnp.cumsum(logf, axis=1).transpose(0, 2, 1)
        attn = forgetting_attention(to_heads(q), to_heads(k), to_heads(v), cum_logf)
        y_fox = attn.transpose(0, 2, 1, 3).reshape(bsz, s, FOX_WIDTH)

        merged = (jax.nn.sigmoid(gate_lru) * (y_lru @ w_lru_out)
                  + jax.nn.sigmoid(gate_fox) * (y_fox @ w_fox_out))
        x = x + merged @ w_o

        x = x + moe_ffn(rmsnorm(x, g_ffn), w_router, b_router, w_gate_up, b_gate_up, w_down, b_down)
    return rmsnorm(x, g_final)


_drawn_inputs = setup_inputs


def setup_inputs(seed=0):
    import zlib

    import numpy as np

    out = dict(_drawn_inputs(seed))
    spreads = {}
    factors = {'b_rg': 26.616, 'b_ig': 25.74, 'b_gate_up': 8.0, 'b_down': 8.0, 'g_final': 20.972}
    for name, (base, spread) in spreads.items():
        noise = np.random.default_rng([zlib.crc32(name.encode()), seed]).standard_normal(out[name].shape)
        drawn = base * np.exp(spread * noise) if base else spread * noise
        out[name] = __import__('jax').numpy.asarray(drawn.astype(out[name].dtype))
    for name, factor in factors.items():
        out[name] = (out[name] * factor).astype(out[name].dtype)
    return out
```

```python
import math
from contextlib import ExitStack

import numpy as np
import concourse.bass as bass
from concourse import mybir

F32 = mybir.dt.float32
I32 = mybir.dt.int32
ALU = mybir.AluOpType
ACT = mybir.ActivationFunctionType
AX = mybir.AxisListType

P = 128
S, D = 256, 1024
TT = S // P
KT = D // P
HEADS, HD = 16, 64
N_EXP, TOP_K, FF = 32, 4, 1024
CONV = 4
RMS_EPS = 1e-6
LRU_C = 8.0
LIMIT, ALPHA = 7.0, 1.702
MASKED = -1e30
BIG = 3.0e38

CC = 256
CHUNK = 2048
RING = 12
SLOTS = 64
ROUNDS = S // SLOTS
PAIRS = N_EXP // 2
GU_CHUNKS, DN_CHUNKS = KT, KT // 2
EXP_CHUNKS = GU_CHUNKS + DN_CHUNKS
assert EXP_CHUNKS == RING

C_LRU, C_K, C_Q, C_V, C_LG, C_GL, C_GF, C_WL, C_WF, C_WO = (4 * i for i in range(10))
MIX_CHUNKS = 40
W_IN_COL = {C_LRU: 0, C_K: 3072, C_Q: 2048, C_V: 4096, C_LG: 1024, C_GL: 5136, C_GF: 6160}
F_COL = 5120
EXP_SHIFT = MIX_CHUNKS % RING


def hybrid_block(nc, x, g_mix, w_in, conv_w, conv_b, w_rg, b_rg, w_ig, b_ig, lru_lambda, b_f,
                 w_lru_out, w_fox_out, w_o, g_ffn, w_router, b_router, w_gate_up, b_gate_up,
                 w_down, b_down, g_final, out):
    ctx = ExitStack()
    with ctx:
        def sb(name, shape, dt=F32):
            return ctx.enter_context(nc.sbuf_tensor(name, shape, dt))

        def bank(name):
            return ctx.enter_context(nc.psum_tensor(name, [P, 512], F32))

        def sem(name):
            return ctx.enter_context(nc.semaphore(name))

        ring = sb("ring", [P, RING, CHUNK])
        x_sb = sb("x_sb", [P, TT, D])
        hT = sb("hT", [P, KT, S])
        lru_pad = sb("lru_pad", [P, KT, S + CONV - 1])
        XC = sb("XC", [P, KT, S])
        R = sb("R", [P, KT, S])
        I = sb("I", [P, KT, S])
        LG = sb("LG", [P, KT, S])
        Q = sb("Q", [P, KT, S])
        K = sb("K", [P, KT, S])
        V = sb("V", [P, TT, D])
        GL = sb("GL", [P, KT, S])
        GF = sb("GF", [P, KT, S])
        L = sb("L", [P, 2, 3 * P])
        PT = sb("PT", [P, 2, 3 * P])
        causal = sb("causal", [P, 3 * P])
        ident = sb("ident", [P, P])
        rows = sb("rows", [72, P])
        vec = sb("vec", [P, 72])
        wf = sb("wf", [P, KT, HEADS])
        wr = sb("wr", [P, KT, N_EXP])
        neg8 = sb("neg8", [HEADS, HEADS])
        iota = sb("iota", [P, SLOTS])
        stat = sb("stat", [P, 64])
        lam = sb("lam", [P, 5, KT])
        bf = sb("bf", [HEADS, 1])
        brt = sb("brt", [P, N_EXP])
        epsc = sb("epsc", [P, 1])
        flag = sb("flag", [1, 4])
        cumf = sb("cumf", [HEADS, S])
        flag_i = sb("flag_i", [1, 1], I32)

        def flat(t):
            return t[:, :, :].rearrange("p a b -> p (a b)")

        wrg_bd = flat(GL)[:, 0:1024].rearrange("p (j o) -> p j o", j=KT)
        wig_bd = flat(GL)[:, 1024:2048].rearrange("p (j o) -> p j o", j=KT)
        fz = flat(GF)[0:HEADS, 0:2048].rearrange("p (n s) -> p n s", n=8)
        mg = flat(lru_pad)[:, 0:2048].rearrange("p (j s) -> p j s", j=KT)
        mult = mg
        xs = flat(K).rearrange("p (t d) -> p t d", t=TT)
        one_t = flat(GF).rearrange("p (j s) -> p j s", j=KT)
        tmp = I[:, 0:2, :]

        h2 = flat(hT).rearrange("p (t d) -> p t d", t=TT)
        h2T = Q
        bgu = flat(K)[0:N_EXP, :]
        gffn_b = flat(R)[:, 0:1024]
        gfin_b = flat(R)[:, 1024:2048]
        bdn = flat(LG)[0:N_EXP, 0:1024]
        yT = flat(LG)[:, 1024:2048].rearrange("p (j s) -> p j s", j=KT)
        Y = flat(V)[:, 0:1024]
        gate = flat(V)[:, 1024:1536].rearrange("p (f s) -> p f s", f=KT)
        sig = flat(V)[:, 1536:2048].rearrange("p (f s) -> p f s", f=KT)
        up = flat(I)[:, 0:512].rearrange("p (f s) -> p f s", f=KT)
        glu = flat(I)[:, 512:1024].rearrange("p (f s) -> p f s", f=KT)
        actT = flat(I)[:, 1024:2048].rearrange("p (i f s) -> p i f s", i=2, f=KT)
        hg = flat(GL)[:, 0:1024].rearrange("p (i k s) -> p i k s", i=2, k=KT)
        bguT = flat(GL)[:, 1024:1536].rearrange("p (f e) -> p f e", e=N_EXP)
        selWT = flat(GL)[:, 1536:1792]
        sel = flat(XC)[:, 0:256].rearrange("p (t i s) -> p t i s", t=TT, i=2)
        selW = flat(XC)[:, 256:512].rearrange("p (t i s) -> p t i s", t=TT, i=2)
        EW = N_EXP + TOP_K
        lg = flat(XC)[:, 512:512 + TT * EW].rearrange("p (t e) -> p t e", t=TT)
        rep = flat(XC)[:, 640:640 + TT * EW].rearrange("p (t e) -> p t e", t=TT)
        top8 = flat(XC)[:, 720:736].rearrange("p (t e) -> p t e", t=TT)
        msk = flat(XC)[:, 768:832].rearrange("p (t e) -> p t e", t=TT)
        expw = flat(XC)[:, 832:896].rearrange("p (t e) -> p t e", t=TT)
        comb = flat(XC)[:, 896:896 + TT * EW].rearrange("p (t e) -> p t e", t=TT)
        pos = flat(XC)[:, 1024:1024 + TT * EW].rearrange("p (t e) -> p t e", t=TT)
        tri = flat(XC)[:, 1152:1280]
        ones = flat(XC)[:, 1280:1408]
        combT = flat(XC)[0:N_EXP, 1408:1664]
        yo = flat(hT).rearrange("p (t d) -> p t d", t=TT)

        pj = [bank("pj0"), bank("pj1")]
        ps = [bank("s0"), bank("s1")]
        pt, po = bank("pt"), bank("po")
        ga, gb = bank("ga"), bank("gb")
        ob = [po, ga]
        acc = [[ps[0], ps[1]], [pt, po]]

        loaded = [sem(f"slot{i}_loaded") for i in range(RING)]
        x_loaded, rows_loaded, gatew_loaded, small_loaded, late_loaded = (
            sem(n) for n in ("x_loaded", "rows_loaded", "gatew_loaded", "small_loaded", "late_loaded"))
        ident_ready, causal_ready, neg8_ready, iota_ready, tri_ready, ones_ready, gatew_zeroed = (
            sem(n) for n in ("ident_ready", "causal_ready", "neg8_ready", "iota_ready", "tri_ready", "ones_ready",
                             "gatew_zeroed"))
        gp_step, act_step, dve_step = sem("gp_step"), sem("act_step"), sem("dve_step")
        chunk_done = sem("chunk_done")
        act_evac, dve_evac = sem("act_evac"), sem("dve_evac")
        eps_ready, sumsq_ready, rms_ready, xs_ready, vec_psum, vec_ready, hT_psum, hT_ready = (
            sem(n) for n in ("eps_ready", "sumsq_ready", "rms_ready", "xs_ready", "vec_psum", "vec_ready", "hT_psum",
                             "hT_ready"))
        pad_ready, conv_ready, gates_psum, ri_ready, loga_ready, tanh_ready, a_ready, mult2_ready, mult_ready = (
            sem(n) for n in ("pad_ready", "conv_ready", "gates_psum", "ri_ready", "loga_ready", "tanh_ready", "a_ready",
                             "mult2_ready", "mult_ready"))
        lam_abs, lam_exp, gelu_ready, gl_ready, gf_ready, ylru_ready, merged_ready = (
            sem(n) for n in ("lam_abs", "lam_exp", "gelu_ready", "gl_ready", "gf_ready", "ylru_ready", "merged_ready"))
        f_psum, f_exp, cum_ready, s_psum, logits_ready, exp_ready, p_ready, pt_psum, pt_ready, o_psum, o_evac = (
            sem(n) for n in ("f_psum", "f_exp", "cum_ready", "s_psum", "logits_ready", "exp_ready", "p_ready", "pt_psum",
                             "pt_ready", "o_psum", "o_evac"))
        sumsq2, rms2, h2_ready, h2T_psum, h2T_act, h2T_dve, router_psum, neg_top, exp_top, mask_ready, pos_psum = (
            sem(n) for n in ("sumsq2", "rms2", "h2_ready", "h2T_psum", "h2T_act", "h2T_dve", "router_psum", "neg_top",
                             "exp_top", "mask_ready", "pos_psum"))
        bguT_psum, bguT_ready, comb_ready, combT_psum, combT_ready, maxp_ready, maxT_psum, flag_ready = (
            sem(n) for n in ("bguT_psum", "bguT_ready", "comb_ready", "combT_psum", "combT_ready", "maxp_ready",
                             "maxT_psum", "flag_ready"))
        sel_ready, gathered, hg_ready, gate_ready, sig_ready, act_ready = (
            sem(n) for n in ("sel_ready", "gathered", "hg_ready", "gate_ready", "sig_ready", "act_ready"))
        selw_transposed, selwt_ready, yT_ready, y_transposed, y_ready, scattered, moe_step = (
            sem(n) for n in ("selw_transposed", "selwt_ready", "yT_ready", "y_transposed", "y_ready",
                             "scattered", "moe_step"))
        moe_round = sem("moe_round")
        y_summed, sumsq3, rms3, final_ready, out_stored = (
            sem(n) for n in ("y_summed", "sumsq3", "rms3", "final_ready", "out_stored"))

        block = ctx.enter_context(nc.Block())

        def mixer_chunk_src(c):
            g = c // 4 * 4
            if g in W_IN_COL:
                w, col = w_in, W_IN_COL[g] + (c - g) * CC
            else:
                w, col = {C_WL: w_lru_out, C_WF: w_fox_out, C_WO: w_o}[g], (c - g) * CC
            return w[:, col:col + CC].rearrange("(k p) n -> p k n", p=P)

        @block.sync
        def _(sp):
            sp.dma_start(x_sb[:, :, :], x[0, :, :].rearrange("(t p) d -> p t d", p=P)).then_inc(x_loaded, 16)
            for c in range(MIX_CHUNKS):
                if c >= RING:
                    sp.wait_ge(chunk_done, c - RING + 1)
                sp.dma_start(ring[:, c % RING, :].rearrange("p (k n) -> p k n", k=KT),
                             mixer_chunk_src(c)).then_inc(loaded[c % RING], 16)

            def load_expert(e, first):
                for c in range(EXP_CHUNKS):
                    slot = (EXP_SHIFT + c) % RING
                    sp.wait_ge(chunk_done, first + (c - RING + 1))
                    if c < GU_CHUNKS:
                        src = w_gate_up[bass.ds(e, 1), c * P:(c + 1) * P, :].rearrange("e p n -> p (e n)")
                        dst = ring[:, slot, :]
                    else:
                        j = c - GU_CHUNKS
                        src = w_down[bass.ds(e, 1), 2 * j * P:2 * (j + 1) * P, :].rearrange("e (i p) n -> p (e i) n", p=P)
                        dst = ring[:, slot, :].rearrange("p (i n) -> p i n", i=2)
                    sp.dma_start(dst, src).then_inc(loaded[slot], 16)

            with sp.Fori(0, N_EXP) as e:
                load_expert(e, e * EXP_CHUNKS + MIX_CHUNKS)
            sp.wait_ge(flag_ready, 1)
            over = sp.value_load(flag_i[0:1, 0:1], min_val=0, max_val=1)
            with sp.If(over > 0):
                with sp.Fori(1, ROUNDS) as r:
                    with sp.Fori(0, N_EXP) as e:
                        load_expert(e, r * (N_EXP * EXP_CHUNKS) + e * EXP_CHUNKS + MIX_CHUNKS)
            sp.end_ifs()
            for t in range(TT):
                sp.wait_ge(final_ready, t + 1)
                sp.dma_start(out[0, t * P:(t + 1) * P, :], yo[:, t, :]).then_inc(out_stored, 16)
            sp.wait_ge(out_stored, 16 * TT)

        @block.gpsimd
        def _(g):
            steps = [0]

            def link(ins):
                steps[0] += 1
                ins.then_inc(gp_step, 1)
                g.wait_ge(gp_step, steps[0])

            link(g.memset(ident[:, :], 0.0))
            g.affine_select(out=ident[:, :], in_=ident[:, :], compare_op=ALU.not_equal, fill=1.0, base=0,
                            pattern=[[-1, P]], channel_multiplier=1).then_inc(ident_ready, 1)
            g.memset(flat(GL), 0.0).then_inc(gatew_zeroed, 1)
            g.wait_ge(gatew_zeroed, 1)
            for w, bd in ((w_rg, wrg_bd), (w_ig, wig_bd)):
                v = w.rearrange("(j two) i o -> two i j o", two=2)
                for h in range(2):
                    g.dma_start(bd[HD * h:HD * h + HD, :, HD * h:HD * h + HD], v[h]).then_inc(gatew_loaded, 16)
            link(g.memset(causal[:, :], 0.0))
            for k0 in (0, 2 * P):
                g.affine_select(out=causal[:, k0:k0 + P], in_=causal[:, k0:k0 + P], compare_op=ALU.is_ge, fill=MASKED,
                                base=0, pattern=[[-1, P]], channel_multiplier=1).then_inc(causal_ready, 1)
            link(g.memset(neg8[:, :], 0.0))
            g.affine_select(out=neg8[:, :], in_=neg8[:, :], compare_op=ALU.not_equal, fill=-math.sqrt(HD), base=0,
                            pattern=[[-1, HEADS]], channel_multiplier=1).then_inc(neg8_ready, 1)
            g.iota(iota[:, :], pattern=[[1, SLOTS]], base=0, channel_multiplier=0,
                   allow_small_or_imprecise_dtypes=True).then_inc(iota_ready, 1)
            g.wait_ge(ylru_ready, 1)
            g.dma_start(gffn_b, g_ffn.rearrange("(a n) -> a n", a=1).broadcast_to([P, D])).then_inc(late_loaded, 16)
            g.dma_start(gfin_b, g_final.rearrange("(a n) -> a n", a=1).broadcast_to([P, D])).then_inc(late_loaded, 16)
            g.dma_start(bdn, b_down[:, :]).then_inc(late_loaded, 16)
            g.wait_ge(s_psum, HEADS)
            g.dma_start(bgu, b_gate_up[:, :]).then_inc(late_loaded, 16)
            g.wait_ge(chunk_done, C_WL + 4)
            g.memset(ones, 1.0).then_inc(ones_ready, 1)
            g.wait_ge(ones_ready, 1)
            g.affine_select(out=tri, in_=ones, compare_op=ALU.is_gt, fill=0.0, base=0,
                            pattern=[[1, P]], channel_multiplier=-1).then_inc(tri_ready, 1)

        @block.scalar
        def _(act):
            for src, r0 in ((g_mix, 0), (conv_b, 40), (b_rg, 48), (b_ig, 56), (lru_lambda, 64)):
                act.dma_start(rows[r0:r0 + KT, :], src.rearrange("(j p) -> j p", p=P)).then_inc(rows_loaded, 16)
            act.dma_start(rows[8:40, :], conv_w.rearrange("w (j p) -> (w j) p", p=P)).then_inc(rows_loaded, 16)
            act.dma_start(wf[:, :, :], w_in[:, F_COL:F_COL + HEADS].rearrange("(k p) n -> p k n", p=P)).then_inc(small_loaded, 16)
            act.dma_start(bf[:, :], b_f.rearrange("(h a) -> h a", a=1)).then_inc(small_loaded, 16)
            act.dma_start(wr[:, :, :], w_router.rearrange("(k p) n -> p k n", p=P)).then_inc(small_loaded, 16)
            act.dma_start(brt[:, :], b_router.rearrange("(a n) -> a n", a=1).broadcast_to([P, N_EXP])).then_inc(small_loaded, 16)
            steps = [0]

            def link(ins):
                steps[0] += 1
                ins.then_inc(act_step, 1)
                act.wait_ge(act_step, steps[0])

            act.wait_ge(x_loaded, 16)
            for t in range(TT):
                act.activation(lru_pad[:, 4 * t:4 * t + 4, 0:S], x_sb[:, t, :].rearrange("p (a b) -> p a b", a=4), ACT.Square,
                               accum_out=stat[:, t:t + 1]).then_inc(sumsq_ready, 1)
            act.wait_ge(sumsq_ready, TT)
            act.wait_ge(eps_ready, 1)
            act.activation(stat[:, 2:4], stat[:, 0:2], ACT.Sqrt, scale=1.0 / D, bias=epsc[:, 0:1]).then_inc(rms_ready, 1)

            def evac(c):
                g, j = c // 4 * 4, c % 4
                act.wait_ge(chunk_done, c + 1)
                src = pj[c % 2][:, :].rearrange("p (a s) -> p a s", a=2)
                if g == C_V:
                    dst = V[:, :, j * CC:(j + 1) * CC]
                elif g == C_LRU:
                    dst = lru_pad[:, 2 * j:2 * j + 2, CONV - 1:]
                else:
                    dst = {C_K: K, C_Q: Q, C_LG: LG, C_GL: GL, C_GF: GF}[g][:, 2 * j:2 * j + 2, :]
                act.activation(dst, src, ACT.Identity).then_inc(act_evac, 1)

            for c in range(4):
                evac(c)
            act.wait_ge(f_psum, 1)
            act.wait_ge(small_loaded, 64)
            link(act.activation(fz[:, 0, :], ga[0:HEADS, 0:S], ACT.Identity, bias=bf[:, 0:1]))
            link(act.activation(fz[:, 1, :], fz[:, 0, :], ACT.Abs))
            act.activation(fz[:, 2, :], fz[:, 1, :], ACT.Exp, scale=-1.0).then_inc(f_exp, 1)
            act.wait_ge(lam_abs, 1)
            act.activation(lam[:, 1, :], lam[:, 0, :], ACT.Exp, scale=-1.0).then_inc(lam_exp, 1)
            for c in range(4, 8):
                evac(c)
            for j in range(KT):
                evac(8 + j)
                act.wait_ge(gates_psum, j + 1)
                b = (ga, gb)[j % 2]
                act.activation(R[:, j, :], b[:, 0:S], ACT.Sigmoid, bias=vec[:, 48 + j:49 + j]).then_inc(ri_ready, 1)
                act.activation(I[:, j, :], b[:, S:2 * S], ACT.Sigmoid, bias=vec[:, 56 + j:57 + j]).then_inc(ri_ready, 1)
            act.wait_ge(loga_ready, KT)
            act.activation(mult, R[:, :, :], ACT.Tanh).then_inc(tanh_ready, 1)
            act.wait_ge(tanh_ready, 1)
            act.activation(R[:, :, :], R[:, :, :], ACT.Exp).then_inc(a_ready, 1)
            act.wait_ge(mult2_ready, 1)
            act.activation(mult, mult, ACT.Sqrt).then_inc(mult_ready, 1)

            for s in range(HEADS + 2):
                if s < HEADS:
                    act.wait_ge(logits_ready, s + 1)
                    for q, (lo, hi) in enumerate(((0, P), (P, 3 * P))):
                        n = 2 * (s % 2) + q
                        act.activation(L[:, s % 2, lo:hi], L[:, s % 2, lo:hi], ACT.Exp, scale=1 / math.sqrt(HD),
                                       bias=stat[:, 8 + n:9 + n], accum_out=stat[:, 12 + n:13 + n]).then_inc(exp_ready, 1)
                if s < 12:
                    evac(16 + s)
                if s % 2 == 0 and s >= 4:
                    j = s // 2 - 2
                    act.wait_ge(o_psum, 2 * j + 2)
                    act.activation(Q[:, j, :], ob[j % 2][:, 0:S], ACT.Identity).then_inc(o_evac, 1)
                if s == 7:
                    act.wait_ge(act_evac, C_GL + 4)
                    act.activation(LG[:, :, :], LG[:, :, :], ACT.Gelu_apprx_tanh).then_inc(gelu_ready, 1)
                    act.activation(GL[:, :, :], GL[:, :, :], ACT.Sigmoid).then_inc(gl_ready, 1)
            act.wait_ge(o_psum, HEADS)
            act.activation(Q[:, KT - 1, :], ob[1][:, 0:S], ACT.Identity).then_inc(o_evac, 1)
            act.wait_ge(act_evac, C_GF + 4)
            act.activation(GF[:, :, :], GF[:, :, :], ACT.Sigmoid).then_inc(gf_ready, 1)

            act.wait_ge(dve_evac, MIX_CHUNKS - C_WL)
            for t in range(TT):
                act.activation(flat(GL)[:, 0:D], x_sb[:, t, :], ACT.Square, accum_out=stat[:, 20 + t:21 + t]).then_inc(sumsq2, 1)
                act.wait_ge(sumsq2, t + 1)
            act.activation(stat[:, 22:24], stat[:, 20:22], ACT.Sqrt, scale=1.0 / D, bias=epsc[:, 0:1]).then_inc(rms2, 1)
            for j in (0, 2):
                act.wait_ge(h2T_psum, j + 1)
                act.activation(h2T[:, 2 * j:2 * j + 2, :].rearrange("p a b -> p (a b)"), acc[j // 2][j % 2][:, :],
                               ACT.Identity).then_inc(h2T_act, 1)
            for t in range(TT):
                act.wait_ge(neg_top, 1)
                act.activation(expw[:, t, :], lg[:, t, TOP_K:], ACT.Exp, bias=stat[:, 30 + t:31 + t]).then_inc(exp_top, 1)
            act.wait_ge(combT_psum, 1)
            act.activation(combT, gb[0:N_EXP, 0:S], ACT.Identity).then_inc(combT_ready, 1)

            def expert_round(g0, n0, t0):
                def hg_copy(k, i):
                    act.wait_ge(gathered, k + 1)
                    act.activation(hg[:, i, :, :], ga[:, :].rearrange("p (k s) -> p k s", k=KT),
                                   ACT.Identity).then_inc(hg_ready, 1)

                def sigmoid_of(n):
                    act.wait_ge(gate_ready, n + 1)
                    act.activation(sig, gate, ACT.Sigmoid, scale=ALPHA).then_inc(sig_ready, 1)

                def down_copy(n, i):
                    act.wait_ge(chunk_done, n * EXP_CHUNKS + MIX_CHUNKS + EXP_CHUNKS)
                    act.activation(yT[:, :, i * SLOTS:(i + 1) * SLOTS], gb[:, :].rearrange("p (k s) -> p k s", k=KT),
                                   ACT.Identity).then_inc(yT_ready, 1)

                hg_copy(g0, 0)
                with act.Fori(0, PAIRS) as p:
                    k, n, t = p * 2 + g0 + 1, p * 2 + n0, p + t0
                    sigmoid_of(n)
                    hg_copy(k, 1)
                    act.wait_ge(selw_transposed, t + 1)
                    act.activation(selWT, gb[:, 0:S], ACT.Identity).then_inc(selwt_ready, 1)
                    down_copy(n, 0)
                    sigmoid_of(n + 1)
                    hg_copy(k + 1, 0)
                    down_copy(n + 1, 1)
                    act.wait_ge(y_transposed, t + 1)
                    act.activation(Y[:, 0:512], ga[:, :], ACT.Identity).then_inc(y_ready, 1)

            expert_round(0, 0, 0)
            act.wait_ge(flag_ready, 1)
            over = act.value_load(flag_i[0:1, 0:1], min_val=0, max_val=1)
            with act.If(over > 0):
                with act.Fori(1, ROUNDS) as r:
                    expert_round(r * (N_EXP + 1), r * N_EXP, r * PAIRS)
            act.end_ifs()

            for t in range(TT):
                act.wait_ge(y_summed, 2 * t + 2)
                act.activation(flat(GL)[:, 0:D], yo[:, t, :], ACT.Square, accum_out=stat[:, 40 + t:41 + t]).then_inc(sumsq3, 1)
                act.wait_ge(sumsq3, t + 1)
                act.activation(stat[:, 42 + t:43 + t], stat[:, 40 + t:41 + t], ACT.Sqrt, scale=1.0 / D,
                               bias=epsc[:, 0:1]).then_inc(rms3, 1)

        @block.vector
        def _(dve):
            v = nc.vector
            steps = [0]

            def link(ins):
                steps[0] += 1
                ins.then_inc(dve_step, 1)
                dve.wait_ge(dve_step, steps[0])

            v.memset(epsc[:, :], RMS_EPS).then_inc(eps_ready, 1)
            dve.wait_ge(rms_ready, 1)
            link(v.reciprocal(stat[:, 4:6], stat[:, 2:4]))
            for t in range(TT):
                v.tensor_scalar(xs[:, t, :], x_sb[:, t, :], stat[:, 4 + t:5 + t], None, ALU.mult).then_inc(xs_ready, 1)
            v.memset(lru_pad[:, :, 0:CONV - 1], 0.0).then_inc(pad_ready, 1)
            dve.wait_ge(vec_psum, 1)
            v.tensor_copy(vec[:, :], ga[:, 0:72]).then_inc(vec_ready, 1)
            dve.wait_ge(vec_ready, 1)
            for j in range(KT):
                dve.wait_ge(hT_psum, j // 2 + 1)
                v.tensor_scalar(hT[:, j, :], (ps[0], ps[1], pt, po)[j // 2][:, S * (j % 2):S * (j % 2) + S],
                                vec[:, j:j + 1], None, ALU.mult).then_inc(hT_ready, 1)
            v.scalar_tensor_tensor(lam[:, 0, :], vec[:, 64:72], -1.0, vec[:, 64:72], ALU.mult, ALU.max).then_inc(lam_abs, 1)
            dve.wait_ge(pad_ready, 1)
            for j in range(KT):
                dve.wait_ge(act_evac, C_LRU + j // 2 + 1)
                link(v.tensor_scalar(XC[:, j, :], lru_pad[:, j, 0:S], vec[:, 8 + j:9 + j], vec[:, 40 + j:41 + j],
                                     ALU.mult, ALU.add))
                for i in range(1, CONV):
                    ins = v.scalar_tensor_tensor(XC[:, j, :], lru_pad[:, j, i:i + S], vec[:, 8 + i * KT + j:9 + i * KT + j],
                                                 XC[:, j, :], ALU.mult, ALU.add)
                    if i < CONV - 1:
                        link(ins)
                    else:
                        ins.then_inc(conv_ready, 1)

            def half_log1p(e, y, w, q):
                link(v.tensor_scalar(w, e, 2.0, None, ALU.add))
                link(v.reciprocal(w, w))
                link(v.tensor_tensor(y, e, w, ALU.mult))
                link(v.tensor_tensor(w, y, y, ALU.mult))
                link(v.tensor_scalar(q, w, 1.0 / 15.0, None, ALU.mult))
                for k in (13, 11, 9, 7, 5, 3):
                    link(v.scalar_tensor_tensor(q, q, 1.0 / k, w, ALU.add, ALU.mult))
                link(v.scalar_tensor_tensor(q, q, 1.0, y, ALU.add, ALU.mult))

            dve.wait_ge(lam_exp, 1)
            half_log1p(lam[:, 1, :], lam[:, 2, :], lam[:, 3, :], lam[:, 4, :])
            link(v.tensor_scalar(lam[:, 2, :], vec[:, 64:72], 0.0, LRU_C, ALU.min, ALU.mult))
            link(v.scalar_tensor_tensor(lam[:, 0, :], lam[:, 4, :], -2.0 * LRU_C, lam[:, 2, :], ALU.mult, ALU.add))
            dve.wait_ge(f_exp, 1)
            half_log1p(fz[:, 2, :], fz[:, 3, :], fz[:, 4, :], fz[:, 5, :])
            link(v.tensor_scalar(fz[:, 3, :], fz[:, 0, :], 0.0, None, ALU.min))
            link(v.scalar_tensor_tensor(fz[:, 4, :], fz[:, 5, :], -2.0, fz[:, 3, :], ALU.mult, ALU.add))
            link(v.memset(fz[:, 6, :], 1.0))
            v.tensor_tensor_scan(cumf[:, :], fz[:, 6, :], fz[:, 4, :], 0.0, ALU.mult, ALU.add).then_inc(cum_ready, 1)
            for j in range(KT):
                dve.wait_ge(ri_ready, 2 * j + 1)
                v.tensor_scalar(R[:, j, :], R[:, j, :], lam[:, 0, j:j + 1], None, ALU.mult).then_inc(loga_ready, 1)
            dve.wait_ge(cum_ready, 1)
            dve.wait_ge(tanh_ready, 1)
            link(v.tensor_scalar(one_t, mult, -1.0, 1.0, ALU.mult, ALU.add))
            link(v.reciprocal(one_t, one_t))
            v.scalar_tensor_tensor(mult, mult, -2.0, one_t, ALU.mult, ALU.mult).then_inc(mult2_ready, 1)
            dve.wait_ge(ri_ready, 2 * KT)
            dve.wait_ge(conv_ready, KT)
            link(v.tensor_tensor(I[:, :, :], I[:, :, :], XC[:, :, :], ALU.mult))

            for s in range(HEADS + 2):
                if 1 <= s <= HEADS:
                    b = (s - 1) % 2
                    dve.wait_ge(exp_ready, 2 * s)
                    link(v.reciprocal(stat[:, 16 + 2 * b:18 + 2 * b], stat[:, 12 + 2 * b:14 + 2 * b]))
                    for q, (lo, hi) in enumerate(((0, P), (P, 3 * P))):
                        v.tensor_scalar(L[:, b, lo:hi], L[:, b, lo:hi], stat[:, 16 + 2 * b + q:17 + 2 * b + q], None,
                                        ALU.mult).then_inc(p_ready, 1)
                if s >= 2:
                    dve.wait_ge(pt_psum, s - 1)
                    if s >= 4:
                        dve.wait_ge(o_psum, s - 3)
                    v.tensor_copy(PT[:, s % 2, :], pt[:, 0:3 * P]).then_inc(pt_ready, 1)
                if s < HEADS:
                    if s == 0:
                        dve.wait_ge(causal_ready, 2)
                    dve.wait_ge(s_psum, s + 1)
                    link(v.tensor_tensor(L[:, s % 2, :], ps[s % 2][:, 0:3 * P], causal[:, :], ALU.add))
                    n = 2 * (s % 2)
                    link(v.reduce_max(stat[:, 24:25], L[:, s % 2, 0:P], AX.X))
                    link(v.reduce_max(stat[:, 25:26], L[:, s % 2, P:3 * P], AX.X))
                    v.tensor_scalar(stat[:, 8 + n:10 + n], stat[:, 24:26], -1.0 / math.sqrt(HD), None,
                                    ALU.mult).then_inc(logits_ready, 1)
                    dve.wait_ge(logits_ready, s + 1)
                if s == 0:
                    dve.wait_ge(mult_ready, 1)
                    link(v.tensor_tensor(I[:, :, :], I[:, :, :], mult, ALU.mult))
                if 1 <= s <= KT:
                    dve.wait_ge(a_ready, 1)
                    link(v.tensor_tensor_scan(XC[:, s - 1, :], R[:, s - 1, :], I[:, s - 1, :], 0.0, ALU.mult, ALU.add))
                if s == KT + 1:
                    dve.wait_ge(gelu_ready, 1)
                    v.tensor_tensor(XC[:, :, :], XC[:, :, :], LG[:, :, :], ALU.mult).then_inc(ylru_ready, 1)
                if 12 <= s < HEADS:
                    c = s - 12
                    dve.wait_ge(gl_ready, 1)
                    dve.wait_ge(chunk_done, C_WL + c + 1)
                    v.tensor_tensor(mg[:, 2 * c:2 * c + 2, :], pj[c % 2][:, :].rearrange("p (a s) -> p a s", a=2),
                                    GL[:, 2 * c:2 * c + 2, :], ALU.mult).then_inc(dve_evac, 1)
            dve.wait_ge(bguT_psum, 1)
            v.tensor_copy(bguT, gb[:, :].rearrange("p (f e) -> p f e", e=N_EXP)).then_inc(bguT_ready, 1)
            for c in range(4):
                dve.wait_ge(gf_ready, 1)
                dve.wait_ge(chunk_done, C_WF + c + 1)
                v.tensor_tensor(tmp, pj[c % 2][:, :].rearrange("p (a s) -> p a s", a=2),
                                GF[:, 2 * c:2 * c + 2, :], ALU.mult).then_inc(dve_evac, 1)
                dve.wait_ge(dve_evac, 4 + c + 1)
                v.tensor_tensor(mg[:, 2 * c:2 * c + 2, :], mg[:, 2 * c:2 * c + 2, :], tmp, ALU.add).then_inc(merged_ready, 1)
                dve.wait_ge(merged_ready, c + 1)
            for c in range(4):
                dve.wait_ge(chunk_done, C_WO + c + 1)
                v.tensor_tensor(x_sb[:, :, c * CC:(c + 1) * CC], x_sb[:, :, c * CC:(c + 1) * CC],
                                pj[c % 2][:, :].rearrange("p (a s) -> p a s", a=2), ALU.add).then_inc(dve_evac, 1)

            dve.wait_ge(rms2, 1)
            link(v.reciprocal(stat[:, 26:28], stat[:, 22:24]))
            dve.wait_ge(late_loaded, 64)
            for t in range(TT):
                v.scalar_tensor_tensor(h2[:, t, :], x_sb[:, t, :], stat[:, 26 + t:27 + t], gffn_b, ALU.mult,
                                       ALU.mult).then_inc(h2_ready, 1)
            for j in (1, 3):
                dve.wait_ge(h2T_psum, j + 1)
                v.tensor_copy(h2T[:, 2 * j:2 * j + 2, :].rearrange("p a b -> p (a b)"), acc[j // 2][j % 2][:, :]).then_inc(h2T_dve, 1)

            dve.wait_ge(chunk_done, C_WL + 4)
            link(v.memset(lg[:, :, 0:TOP_K], BIG))
            link(v.memset(pos[:, :, :], -1.0))
            dve.wait_ge(router_psum, 1)
            link(v.tensor_tensor(lg[:, :, TOP_K:], ga[:, 0:TT * N_EXP].rearrange("p (t e) -> p t e", t=TT),
                                 brt[:, :].unsqueeze(1).broadcast_to([P, TT, N_EXP]), ALU.add))
            for t in range(TT):
                link(v.max(top8[:, t, :], lg[:, t, :]))
            v.tensor_scalar(stat[:, 30:32], top8[:, :, TOP_K], -1.0, None, ALU.mult).then_inc(neg_top, 1)
            for t in range(TT):
                link(v.match_replace(rep[:, t, :], top8[:, t, :], lg[:, t, :], -BIG))
            v.tensor_tensor(msk, rep[:, :, TOP_K:], lg[:, :, TOP_K:], ALU.not_equal).then_inc(mask_ready, 1)
            dve.wait_ge(mask_ready, 1)
            dve.wait_ge(exp_top, TT)
            link(v.tensor_tensor(expw, expw, msk, ALU.mult))
            link(v.reduce_sum(stat[:, 32:34], expw, AX.X))
            link(v.reciprocal(stat[:, 34:36], stat[:, 32:34]))
            link(v.memset(comb[:, :, N_EXP:], 0.0))
            v.tensor_tensor(comb[:, :, 0:N_EXP], expw, stat[:, 34:36].unsqueeze(2).broadcast_to([P, TT, N_EXP]),
                            ALU.mult).then_inc(comb_ready, 1)
            dve.wait_ge(comb_ready, 1)
            dve.wait_ge(pos_psum, 1)
            link(v.scalar_tensor_tensor(pos[:, :, 0:N_EXP], ga[:, 256:256 + TT * N_EXP].rearrange("p (t e) -> p t e", t=TT),
                                        1.0, msk, ALU.add, ALU.mult))
            link(v.tensor_scalar(pos[:, :, 0:N_EXP], pos[:, :, 0:N_EXP], -1.0, None, ALU.add))

            def build_sel(p2):
                v.tensor_tensor(sel, iota[:, :].unsqueeze(1).unsqueeze(1).broadcast_to([P, TT, 2, SLOTS]),
                                pos[:, :, bass.ds(p2, 2)].unsqueeze(3).broadcast_to([P, TT, 2, SLOTS]),
                                ALU.is_equal).then_inc(sel_ready, 1)

            def weigh_sel(p2):
                v.tensor_tensor(selW, sel, comb[:, :, bass.ds(p2, 2)].unsqueeze(3).broadcast_to([P, TT, 2, SLOTS]),
                                ALU.mult).then_inc(sel_ready, 1)

            dve.wait_ge(iota_ready, 1)

            def expert_round(b0, g0, n0, t0):
                def glu_of(n, e, i):
                    c0 = n * 4
                    dve.wait_ge(chunk_done, n * EXP_CHUNKS + MIX_CHUNKS + GU_CHUNKS)
                    v.tensor_tensor(gate, pj[0][:, :].rearrange("p (f s) -> p f s", f=KT),
                                    bguT[:, 0:KT, bass.ds(e, 1)].broadcast_to([P, KT, SLOTS]), ALU.add).then_inc(moe_step, 1)
                    v.tensor_tensor(up, pj[1][:, :].rearrange("p (f s) -> p f s", f=KT),
                                    bguT[:, KT:2 * KT, bass.ds(e, 1)].broadcast_to([P, KT, SLOTS]), ALU.add).then_inc(moe_step, 1)
                    dve.wait_ge(moe_step, c0 + 1)
                    v.tensor_scalar(gate, gate, LIMIT, None, ALU.min).then_inc(gate_ready, 1)
                    dve.wait_ge(moe_step, c0 + 2)
                    v.tensor_scalar(up, up, LIMIT, -LIMIT, ALU.min, ALU.max).then_inc(moe_step, 1)
                    dve.wait_ge(gate_ready, n + 1)
                    dve.wait_ge(sig_ready, n + 1)
                    v.tensor_tensor(glu, gate, sig, ALU.mult).then_inc(moe_step, 1)
                    dve.wait_ge(moe_step, c0 + 4)
                    v.scalar_tensor_tensor(actT[:, i, :, :], up, 1.0, glu, ALU.add, ALU.mult).then_inc(act_ready, 1)

                build_sel(0)
                dve.wait_ge(sel_ready, b0 * 2 + 1)
                weigh_sel(0)
                with dve.Fori(0, PAIRS) as p:
                    n, t, e, b = p * 2 + n0, p + t0, p * 2, (p + b0) * 2 + 2
                    glu_of(n, e, 0)
                    dve.wait_ge(gathered, p * 2 + g0 + 2)
                    build_sel(e + 2)
                    dve.wait_ge(selw_transposed, t + 1)
                    dve.wait_ge(sel_ready, b + 1)
                    weigh_sel(e + 2)
                    glu_of(n + 1, e + 1, 1)
                    dve.wait_ge(y_transposed, t + 1)
                    v.tensor_copy(Y[:, 512:1024], gb[:, :]).then_inc(y_ready, 1)

            v.tensor_reduce(stat[:, 36:37], pos[:, :, :], AX.XY, ALU.max).then_inc(maxp_ready, 1)
            dve.wait_ge(maxT_psum, 1)
            link(v.reduce_max(flag[0:1, 0:1], ga[0:1, 384:512], AX.X))
            link(v.tensor_scalar(flag[0:1, 1:2], flag[0:1, 0:1], float(SLOTS) - 0.5, None, ALU.is_gt))
            v.tensor_copy(flag_i[0:1, 0:1], flag[0:1, 1:2]).then_inc(flag_ready, 1)

            expert_round(0, 0, 0, 0)
            dve.wait_ge(scattered, PAIRS)
            dve.wait_ge(flag_ready, 1)
            over = dve.value_load(flag_i[0:1, 0:1], min_val=0, max_val=1)
            with dve.If(over > 0):
                with dve.Fori(1, ROUNDS) as r:
                    dve.wait_ge(gathered, r * (N_EXP + 1))
                    v.tensor_scalar(pos[:, :, 0:N_EXP], pos[:, :, 0:N_EXP], -float(SLOTS), None,
                                    ALU.add).then_inc(moe_round, 1)
                    dve.wait_ge(moe_round, r)
                    expert_round(r * (PAIRS + 1), r * (N_EXP + 1), r * N_EXP, r * PAIRS)
                    dve.wait_ge(scattered, (r + 1) * PAIRS)
            dve.end_ifs()

            for t in range(TT):
                for h in range(2):
                    v.tensor_tensor(yo[:, t, h * 512:(h + 1) * 512], x_sb[:, t, h * 512:(h + 1) * 512], acc[t][h][:, :],
                                    ALU.add).then_inc(y_summed, 1)
            for t in range(TT):
                dve.wait_ge(rms3, t + 1)
                link(v.reciprocal(stat[:, 44 + t:45 + t], stat[:, 42 + t:43 + t]))
                dve.wait_ge(y_summed, 2 * t + 2)
                v.scalar_tensor_tensor(yo[:, t, :], yo[:, t, :], stat[:, 44 + t:45 + t], gfin_b, ALU.mult,
                                       ALU.mult).then_inc(final_ready, 1)

        @block.tensor
        def _(pe):
            mm = nc.tensor.matmul

            pe.wait_ge(ident_ready, 1)
            pe.wait_ge(rows_loaded, 96)
            nc.tensor.transpose(ga[:, 0:72], rows[:, :], ident[0:72, 0:72]).then_inc(vec_psum, 1)
            pe.wait_ge(xs_ready, TT)
            for j in range(KT):
                for t in range(TT):
                    c0 = S * (j % 2) + t * P
                    last = nc.tensor.transpose((ps[0], ps[1], pt, po)[j // 2][:, c0:c0 + P], xs[:, t, j * P:(j + 1) * P], ident[:, :])
                if j % 2:
                    last.then_inc(hT_psum, 1)
            pe.wait_ge(hT_ready, KT)
            pe.wait_ge(vec_ready, 1)
            pe.wait_ge(small_loaded, 64)
            for k in range(KT):
                last = mm(ga[0:HEADS, 0:S], wf[:, k, :], hT[:, k, :], start=(k == 0), stop=(k == KT - 1))
            last.then_inc(f_psum, 1)

            def free_pj(c):
                if c - 2 >= C_WL:
                    pe.wait_ge(dve_evac, c - 1 - C_WL)
                elif c >= 2:
                    pe.wait_ge(act_evac, c - 1)

            def chunk(c):
                w = ring[:, c % RING, :].rearrange("p (k n) -> p k n", k=KT)
                g = c // 4 * 4
                pe.wait_ge(loaded[c % RING], 16 * (c // RING + 1))
                free_pj(c)
                for a in range(2):
                    for k in range(KT):
                        if g == C_V:
                            lhs, rhs = hT[:, k, a * P:(a + 1) * P], w[:, k, :]
                        elif g == C_WO:
                            lhs, rhs = mg[:, k, a * P:(a + 1) * P], w[:, k, :]
                        else:
                            lhs, rhs = w[:, k, a * P:(a + 1) * P], {C_WL: XC, C_WF: Q}.get(g, hT)[:, k, :]
                        last = mm(pj[c % 2][:, a * S:(a + 1) * S], lhs, rhs, start=(k == 0), stop=(k == KT - 1))
                last.then_inc(chunk_done, 1)

            for c in range(8):
                chunk(c)
            for j in range(KT):
                chunk(8 + j)
                if j == 0:
                    pe.wait_ge(gatew_loaded, 64)
                pe.wait_ge(conv_ready, j + 1)
                if j >= 2:
                    pe.wait_ge(ri_ready, 2 * (j - 1))
                else:
                    pe.wait_ge(f_exp, 1)
                b = (ga, gb)[j % 2]
                mm(b[:, 0:S], wrg_bd[:, j, :], XC[:, j, :], start=True, stop=True)
                mm(b[:, S:2 * S], wig_bd[:, j, :], XC[:, j, :], start=True, stop=True).then_inc(gates_psum, 1)

            for s in range(HEADS + 2):
                if s < HEADS:
                    if s == 0:
                        pe.wait_ge(act_evac, C_V + 4)
                        pe.wait_ge(cum_ready, 1)
                        pe.wait_ge(neg8_ready, 1)
                    if s >= 2:
                        pe.wait_ge(logits_ready, s - 1)
                    j, r0 = s // 2, HD * (s % 2)
                    for q, (c0, n) in enumerate(((0, P), (P, 2 * P))):
                        mm(ps[s % 2][:, c0:c0 + n], Q[r0:r0 + HD, j, q * P:(q + 1) * P], K[r0:r0 + HD, j, 0:n],
                           start=True, stop=False)
                        last = mm(ps[s % 2][:, c0:c0 + n], neg8[:, s:s + 1].broadcast_to([HEADS, P]), cumf[:, 0:n],
                                  start=False, stop=True)
                    last.then_inc(s_psum, 1)
                    if 16 + s == C_WL:
                        pe.wait_ge(ylru_ready, 1)
                    chunk(16 + s)
                if 1 <= s <= HEADS:
                    pe.wait_ge(p_ready, 2 * s)
                    if s >= 2:
                        pe.wait_ge(pt_ready, s - 1)
                    for b in range(3):
                        last = nc.tensor.transpose(pt[:, b * P:(b + 1) * P], L[:, (s - 1) % 2, b * P:(b + 1) * P], ident[:, :])
                    last.then_inc(pt_psum, 1)
                if s >= 2:
                    h = s - 2
                    j, r0 = h // 2, HD * (h % 2)
                    pe.wait_ge(pt_ready, h + 1)
                    if j >= 2:
                        pe.wait_ge(o_evac, j - 1)
                    elif j == 1:
                        pe.wait_ge(ri_ready, 2 * KT)
                    o = ob[j % 2][r0:r0 + HD, 0:S]
                    mm(o[:, 0:P], V[:, 0, h * HD:(h + 1) * HD], PT[:, h % 2, 0:P], start=True, stop=True)
                    mm(o[:, P:2 * P], V[:, 0, h * HD:(h + 1) * HD], PT[:, h % 2, P:2 * P], start=True, stop=False)
                    mm(o[:, P:2 * P], V[:, 1, h * HD:(h + 1) * HD], PT[:, h % 2, 2 * P:3 * P], start=False,
                       stop=True).then_inc(o_psum, 1)
            pe.wait_ge(late_loaded, 64)
            for f in range(2 * KT):
                last = nc.tensor.transpose(gb[:, f * N_EXP:(f + 1) * N_EXP], bgu[:, f * P:(f + 1) * P], ident[0:N_EXP, 0:N_EXP])
            last.then_inc(bguT_psum, 1)
            pe.wait_ge(o_evac, KT)
            for c in range(C_WF, C_WF + 4):
                chunk(c)
            pe.wait_ge(merged_ready, 4)
            for c in range(C_WO, C_WO + 4):
                chunk(c)

            pe.wait_ge(h2_ready, TT)
            for j in range(KT):
                for t in range(TT):
                    c0 = S * (j % 2) + t * P
                    last = nc.tensor.transpose(acc[j // 4][j // 2 % 2][:, c0:c0 + P], h2[:, t, j * P:(j + 1) * P], ident[:, :])
                if j % 2:
                    last.then_inc(h2T_psum, 1)
            pe.wait_ge(h2T_act, 2)
            pe.wait_ge(h2T_dve, 2)
            for t in range(TT):
                for k in range(KT):
                    last = mm(ga[:, t * N_EXP:(t + 1) * N_EXP], h2T[:, k, t * P:(t + 1) * P], wr[:, k, :], start=(k == 0),
                              stop=(k == KT - 1))
            last.then_inc(router_psum, 1)
            pe.wait_ge(tri_ready, 1)
            pe.wait_ge(mask_ready, 1)
            mm(ga[:, 256:256 + N_EXP], tri, msk[:, 0, :], start=True, stop=True)
            mm(ga[:, 256 + N_EXP:256 + 2 * N_EXP], ones, msk[:, 0, :], start=True, stop=False)
            mm(ga[:, 256 + N_EXP:256 + 2 * N_EXP], tri, msk[:, 1, :], start=False, stop=True).then_inc(pos_psum, 1)
            pe.wait_ge(comb_ready, 1)
            pe.wait_ge(bguT_ready, 1)
            for t in range(TT):
                last = nc.tensor.transpose(gb[0:N_EXP, t * P:(t + 1) * P], comb[:, t, 0:N_EXP], ident[:, :])
            last.then_inc(combT_psum, 1)
            pe.wait_ge(maxp_ready, 1)
            nc.tensor.transpose(ga[0:1, 384:512], stat[:, 36:37], ident[:, :]).then_inc(maxT_psum, 1)
            pe.wait_ge(combT_ready, 1)
            for t in range(TT):
                for h in range(2):
                    mm(acc[t][h][:, :], combT[:, t * P:(t + 1) * P], bdn[:, h * 512:(h + 1) * 512], start=True, stop=True,
                       skip_group_check=True)
            pe.wait_ge(flag_ready, 1)

            def expert_round(b0, g0, n0, t0):
                def gather(i):
                    for k in range(KT):
                        for t in range(TT):
                            last = mm(ga[:, k * SLOTS:(k + 1) * SLOTS], h2[:, t, k * P:(k + 1) * P], sel[:, t, i, :],
                                      start=(t == 0), stop=(t == TT - 1))
                    last.then_inc(gathered, 1)

                def chunk_here(n, c):
                    slot = (EXP_SHIFT + c) % RING
                    pe.wait_ge(loaded[slot], n * 16 + 16 * (MIX_CHUNKS // RING + 1 + (EXP_SHIFT + c) // RING))
                    return slot

                def gate_up(n, k, i):
                    pe.wait_ge(hg_ready, k)
                    for c in range(GU_CHUNKS):
                        slot = chunk_here(n, c)
                        for f in range(2 * KT):
                            last = mm(pj[f // KT][:, f % KT * SLOTS:(f % KT + 1) * SLOTS], ring[:, slot, f * P:(f + 1) * P],
                                      hg[:, i, c, :], start=(c == 0 and f % KT == 0), stop=(c == GU_CHUNKS - 1),
                                      skip_group_check=True)
                        last.then_inc(chunk_done, 1)

                def down(n, i):
                    pe.wait_ge(act_ready, n + 1)
                    for c in range(DN_CHUNKS):
                        slot = chunk_here(n, GU_CHUNKS + c)
                        for a in range(2):
                            for f in range(KT):
                                last = mm(gb[:, f * SLOTS:(f + 1) * SLOTS], ring[:, slot, a * D + f * P:a * D + (f + 1) * P],
                                          actT[:, i, 2 * c + a, :], start=(c == 0 and a == 0 and f == 0),
                                          stop=(c == DN_CHUNKS - 1 and a == 1), skip_group_check=True)
                        last.then_inc(chunk_done, 1)

                pe.wait_ge(sel_ready, b0 * 2 + 1)
                gather(0)
                with pe.Fori(0, PAIRS) as p:
                    n, t, k = p * 2 + n0, p + t0, p * 2 + g0 + 1
                    gate_up(n, k, 0)
                    gather(1)
                    pe.wait_ge(sel_ready, (p + b0) * 2 + 2)
                    for tt in range(TT):
                        last = nc.tensor.transpose(gb[:, tt * P:(tt + 1) * P], selW[:, tt, :, :].rearrange("p i s -> p (i s)"),
                                                   ident[:, :])
                    last.then_inc(selw_transposed, 1)
                    pe.wait_ge(selwt_ready, t + 1)
                    down(n, 0)
                    gate_up(n + 1, k + 1, 1)
                    pe.wait_ge(sel_ready, (p + b0) * 2 + 3)
                    gather(0)
                    pe.wait_ge(yT_ready, n + 1)
                    down(n + 1, 1)
                    pe.wait_ge(hg_ready, k + 2)
                    pe.wait_ge(yT_ready, n + 2)
                    for j in range(KT):
                        last = nc.tensor.transpose((ga, gb)[j // 4][:, j % 4 * P:(j % 4 + 1) * P], yT[:, j, :], ident[:, :])
                    last.then_inc(y_transposed, 1)
                    pe.wait_ge(y_ready, t * 2 + 2)
                    for tt in range(TT):
                        for h in range(2):
                            last = mm(acc[tt][h][:, :], selWT[:, tt * P:(tt + 1) * P], Y[:, h * 512:(h + 1) * 512],
                                      start=False, stop=True, skip_group_check=True)
                    last.then_inc(scattered, 1)

            expert_round(0, 0, 0, 0)
            over = pe.value_load(flag_i[0:1, 0:1], min_val=0, max_val=1)
            with pe.If(over > 0):
                with pe.Fori(1, ROUNDS) as r:
                    expert_round(r * (PAIRS + 1), r * (N_EXP + 1), r * N_EXP, r * PAIRS)
            pe.end_ifs()


_INS = ["x", "g_mix", "w_in", "conv_w", "conv_b", "w_rg", "b_rg", "w_ig", "b_ig", "lru_lambda", "b_f", "w_lru_out",
        "w_fox_out", "w_o", "g_ffn", "w_router", "b_router", "w_gate_up", "b_gate_up", "w_down", "b_down", "g_final"]


def kernel(**inputs):
    import concourse.bacc as bacc
    from concourse.bass_utils import run_bass_kernel_spmd

    nc = bacc.Bacc("TRN2", target_bir_lowering=False, num_devices=1)
    arrays, args = {}, []
    for name in _INS:
        a = np.ascontiguousarray(inputs[name])
        arrays[f"in_{name}"] = a
        args.append(nc.dram_tensor(f"in_{name}", a.shape, mybir.dt.from_np(a.dtype), kind="ExternalInput").ap())
    out = nc.dram_tensor("out_0", inputs["x"].shape, F32, kind="ExternalOutput").ap()
    hybrid_block(nc, *args, out)
    r = run_bass_kernel_spmd(nc, [arrays], core_ids=[0])
    return r.results[0]["out_0"]
```

```python
import math
from contextlib import ExitStack

import numpy as np
import concourse.bass as bass
from concourse import mybir

F32 = mybir.dt.float32
I32 = mybir.dt.int32
ALU = mybir.AluOpType
ACT = mybir.ActivationFunctionType
AX = mybir.AxisListType

P = 128
S, D = 256, 1024
TT = S // P
KT = D // P
HEADS, HD = 16, 64
N_EXP, TOP_K, FF = 32, 4, 1024
CONV = 4
RMS_EPS = 1e-6
LRU_C = 8.0
LIMIT, ALPHA = 7.0, 1.702
MASKED = -1e30
BIG = 3.0e38

CC = 256
CHUNK = 2048
RING = 12
SLOTS = 64
ROUNDS = S // SLOTS
PAIRS = N_EXP // 2
GU_CHUNKS, DN_CHUNKS = KT, KT // 2
EXP_CHUNKS = GU_CHUNKS + DN_CHUNKS
assert EXP_CHUNKS == RING

C_LRU, C_K, C_Q, C_V, C_LG, C_GL, C_GF, C_WL, C_WF, C_WO = (4 * i for i in range(10))
MIX_CHUNKS = 40
W_IN_COL = {C_LRU: 0, C_K: 3072, C_Q: 2048, C_V: 4096, C_LG: 1024, C_GL: 5136, C_GF: 6160}
F_COL = 5120
EXP_SHIFT = MIX_CHUNKS % RING


def hybrid_block(nc, x, g_mix, w_in, conv_w, conv_b, w_rg, b_rg, w_ig, b_ig, lru_lambda, b_f,
                 w_lru_out, w_fox_out, w_o, g_ffn, w_router, b_router, w_gate_up, b_gate_up,
                 w_down, b_down, g_final, out):
    ctx = ExitStack()
    with ctx:
        def sb(name, shape, dt=F32):
            return ctx.enter_context(nc.sbuf_tensor(name, shape, dt))

        def bank(name):
            return ctx.enter_context(nc.psum_tensor(name, [P, 512], F32))

        def sem(name):
            return ctx.enter_context(nc.semaphore(name))

        ring = sb("ring", [P, RING, CHUNK])
        x_sb = sb("x_sb", [P, TT, D])
        hT = sb("hT", [P, KT, S])
        lru_pad = sb("lru_pad", [P, KT, S + CONV - 1])
        XC = sb("XC", [P, KT, S])
        R = sb("R", [P, KT, S])
        I = sb("I", [P, KT, S])
        LG = sb("LG", [P, KT, S])
        Q = sb("Q", [P, KT, S])
        K = sb("K", [P, KT, S])
        V = sb("V", [P, TT, D])
        GL = sb("GL", [P, KT, S])
        GF = sb("GF", [P, KT, S])
        L = sb("L", [P, 2, 3 * P])
        PT = sb("PT", [P, 2, 3 * P])
        causal = sb("causal", [P, 3 * P])
        ident = sb("ident", [P, P])
        rows = sb("rows", [72, P])
        vec = sb("vec", [P, 72])
        wf = sb("wf", [P, KT, HEADS])
        wr = sb("wr", [P, KT, N_EXP])
        neg8 = sb("neg8", [HEADS, HEADS])
        iota = sb("iota", [P, 2, SLOTS])
        stat = sb("stat", [P, 64])
        lam = sb("lam", [P, 5, KT])
        bf = sb("bf", [HEADS, 1])
        brt = sb("brt", [P, N_EXP])
        epsc = sb("epsc", [P, 1])
        flag = sb("flag", [1, 4])
        cumf = sb("cumf", [HEADS, S])
        flag_i = sb("flag_i", [1, 1], I32)

        def flat(t):
            return t[:, :, :].rearrange("p a b -> p (a b)")

        wrg_bd = flat(GL)[:, 0:1024].rearrange("p (j o) -> p j o", j=KT)
        wig_bd = flat(GL)[:, 1024:2048].rearrange("p (j o) -> p j o", j=KT)
        fz = flat(GF)[0:HEADS, 0:2048].rearrange("p (n s) -> p n s", n=8)
        mg = flat(lru_pad)[:, 0:2048].rearrange("p (j s) -> p j s", j=KT)
        mult = mg
        xs = flat(K).rearrange("p (t d) -> p t d", t=TT)
        one_t = flat(GF).rearrange("p (j s) -> p j s", j=KT)
        tmp = I[:, 0:2, :]

        h2 = flat(hT).rearrange("p (t d) -> p t d", t=TT)
        h2T = Q
        bgu = flat(K)[0:N_EXP, :]
        gffn_b = flat(R)[:, 0:1024]
        gfin_b = flat(R)[:, 1024:2048]
        bdn = flat(LG)[0:N_EXP, 0:1024]
        gate = flat(V)[:, 0:512]
        sig = flat(V)[:, 512:1024]
        up = flat(V)[:, 1024:1536]
        glu = flat(V)[:, 1536:2048]
        prod = flat(I)[:, 0:512]
        Y = flat(I)[:, 512:1024]
        actT = flat(I)[:, 1024:1536].rearrange("p (j h s) -> p j h s", h=2, s=SLOTS)
        hg = flat(GL)[:, 0:1024].rearrange("p (k i s) -> p k i s", k=KT, i=2)
        selWT = flat(GL)[:, 1024:1536].rearrange("p (i n) -> p i n", i=2)
        onehot = flat(GL)[0:N_EXP, 1536:1664].rearrange("p (i s) -> p i s", i=2)
        sel = flat(LG)[:, 1024:1536].rearrange("p (t i s) -> p t i s", t=TT, i=2)
        selW = flat(LG)[:, 1536:2048].rearrange("p (t i s) -> p t i s", t=TT, i=2)
        EW = N_EXP + TOP_K
        lg = flat(XC)[:, 512:512 + TT * EW].rearrange("p (t e) -> p t e", t=TT)
        rep = flat(XC)[:, 640:640 + TT * EW].rearrange("p (t e) -> p t e", t=TT)
        top8 = flat(XC)[:, 720:736].rearrange("p (t e) -> p t e", t=TT)
        msk = flat(XC)[:, 768:832].rearrange("p (t e) -> p t e", t=TT)
        expw = flat(XC)[:, 832:896].rearrange("p (t e) -> p t e", t=TT)
        comb = flat(XC)[:, 896:896 + TT * EW].rearrange("p (t e) -> p t e", t=TT)
        pos = flat(XC)[:, 1024:1024 + TT * EW].rearrange("p (t e) -> p t e", t=TT)
        tri = flat(XC)[:, 1152:1280]
        ones = flat(XC)[:, 1280:1408]
        combT = flat(XC)[0:N_EXP, 1408:1664]
        yo = flat(hT).rearrange("p (t d) -> p t d", t=TT)

        pj = [bank("pj0"), bank("pj1")]
        ps = [bank("s0"), bank("s1")]
        pt, po = bank("pt"), bank("po")
        ga, gb = bank("ga"), bank("gb")
        ob = [po, ga]
        acc = [[ps[0], ps[1]], [pt, po]]

        loaded = [sem(f"slot{i}_loaded") for i in range(RING)]
        x_loaded, rows_loaded, gatew_loaded, small_loaded, late_loaded = (
            sem(n) for n in ("x_loaded", "rows_loaded", "gatew_loaded", "small_loaded", "late_loaded"))
        ident_ready, causal_ready, neg8_ready, iota_ready, tri_ready, ones_ready, gatew_zeroed = (
            sem(n) for n in ("ident_ready", "causal_ready", "neg8_ready", "iota_ready", "tri_ready", "ones_ready",
                             "gatew_zeroed"))
        gp_step, act_step, dve_step = sem("gp_step"), sem("act_step"), sem("dve_step")
        chunk_done = sem("chunk_done")
        act_evac, dve_evac = sem("act_evac"), sem("dve_evac")
        eps_ready, sumsq_ready, rms_ready, xs_ready, vec_psum, vec_ready, hT_psum, hT_ready = (
            sem(n) for n in ("eps_ready", "sumsq_ready", "rms_ready", "xs_ready", "vec_psum", "vec_ready", "hT_psum",
                             "hT_ready"))
        pad_ready, conv_ready, gates_psum, ri_ready, loga_ready, tanh_ready, a_ready, mult2_ready, mult_ready = (
            sem(n) for n in ("pad_ready", "conv_ready", "gates_psum", "ri_ready", "loga_ready", "tanh_ready", "a_ready",
                             "mult2_ready", "mult_ready"))
        lam_abs, lam_exp, gelu_ready, gl_ready, gf_ready, ylru_ready, merged_ready = (
            sem(n) for n in ("lam_abs", "lam_exp", "gelu_ready", "gl_ready", "gf_ready", "ylru_ready", "merged_ready"))
        f_psum, f_exp, cum_ready, s_psum, logits_ready, exp_ready, p_ready, pt_psum, pt_ready, o_psum, o_evac = (
            sem(n) for n in ("f_psum", "f_exp", "cum_ready", "s_psum", "logits_ready", "exp_ready", "p_ready", "pt_psum",
                             "pt_ready", "o_psum", "o_evac"))
        sumsq2, rms2, h2_ready, h2T_psum, h2T_act, h2T_dve, router_psum, neg_top, exp_top, mask_ready, pos_psum = (
            sem(n) for n in ("sumsq2", "rms2", "h2_ready", "h2T_psum", "h2T_act", "h2T_dve", "router_psum", "neg_top",
                             "exp_top", "mask_ready", "pos_psum"))
        comb_ready, combT_psum, combT_ready, maxp_ready, maxT_psum, flag_ready = (
            sem(n) for n in ("comb_ready", "combT_psum", "combT_ready", "maxp_ready",
                             "maxT_psum", "flag_ready"))
        sel_ready, onehot_ready, gathered, hg_ready, gate_ready, sig_ready, act_ready = (
            sem(n) for n in ("sel_ready", "onehot_ready", "gathered", "hg_ready", "gate_ready", "sig_ready", "act_ready"))
        selw_transposed, selwt_ready, act_transposed, actT_ready, y_ready, scattered, moe_step = (
            sem(n) for n in ("selw_transposed", "selwt_ready", "act_transposed", "actT_ready", "y_ready",
                             "scattered", "moe_step"))
        moe_round = sem("moe_round")
        y_summed, sumsq3, rms3, final_ready, out_stored = (
            sem(n) for n in ("y_summed", "sumsq3", "rms3", "final_ready", "out_stored"))

        block = ctx.enter_context(nc.Block())

        def mixer_chunk_src(c):
            g = c // 4 * 4
            if g in W_IN_COL:
                w, col = w_in, W_IN_COL[g] + (c - g) * CC
            else:
                w, col = {C_WL: w_lru_out, C_WF: w_fox_out, C_WO: w_o}[g], (c - g) * CC
            return w[:, col:col + CC].rearrange("(k p) n -> p k n", p=P)

        @block.sync
        def _(sp):
            sp.dma_start(x_sb[:, :, :], x[0, :, :].rearrange("(t p) d -> p t d", p=P)).then_inc(x_loaded, 16)
            for c in range(MIX_CHUNKS):
                if c >= RING:
                    sp.wait_ge(chunk_done, c - RING + 1)
                sp.dma_start(ring[:, c % RING, :].rearrange("p (k n) -> p k n", k=KT),
                             mixer_chunk_src(c)).then_inc(loaded[c % RING], 16)

            def load_expert(e, first):
                for c in range(EXP_CHUNKS):
                    slot = (EXP_SHIFT + c) % RING
                    sp.wait_ge(chunk_done, first + (c - RING + 1))
                    if c < GU_CHUNKS:
                        src = w_gate_up[bass.ds(e, 1), c * P:(c + 1) * P, :].rearrange("e p n -> p (e n)")
                        dst = ring[:, slot, :]
                    else:
                        j = c - GU_CHUNKS
                        src = w_down[bass.ds(e, 1), 2 * j * P:2 * (j + 1) * P, :].rearrange("e (i p) n -> p (e i) n", p=P)
                        dst = ring[:, slot, :].rearrange("p (i n) -> p i n", i=2)
                    sp.dma_start(dst, src).then_inc(loaded[slot], 16)

            with sp.Fori(0, N_EXP) as e:
                load_expert(e, e * EXP_CHUNKS + MIX_CHUNKS)
            sp.wait_ge(flag_ready, 1)
            over = sp.value_load(flag_i[0:1, 0:1], min_val=0, max_val=1)
            with sp.If(over > 0):
                with sp.Fori(1, ROUNDS) as r:
                    with sp.Fori(0, N_EXP) as e:
                        load_expert(e, r * (N_EXP * EXP_CHUNKS) + e * EXP_CHUNKS + MIX_CHUNKS)
            sp.end_ifs()
            for t in range(TT):
                sp.wait_ge(final_ready, t + 1)
                sp.dma_start(out[0, t * P:(t + 1) * P, :], yo[:, t, :]).then_inc(out_stored, 16)
            sp.wait_ge(out_stored, 16 * TT)

        @block.gpsimd
        def _(g):
            steps = [0]

            def link(ins):
                steps[0] += 1
                ins.then_inc(gp_step, 1)
                g.wait_ge(gp_step, steps[0])

            link(g.memset(ident[:, :], 0.0))
            g.affine_select(out=ident[:, :], in_=ident[:, :], compare_op=ALU.not_equal, fill=1.0, base=0,
                            pattern=[[-1, P]], channel_multiplier=1).then_inc(ident_ready, 1)
            g.memset(flat(GL), 0.0).then_inc(gatew_zeroed, 1)
            g.wait_ge(gatew_zeroed, 1)
            for w, bd in ((w_rg, wrg_bd), (w_ig, wig_bd)):
                v = w.rearrange("(j two) i o -> two i j o", two=2)
                for h in range(2):
                    g.dma_start(bd[HD * h:HD * h + HD, :, HD * h:HD * h + HD], v[h]).then_inc(gatew_loaded, 16)
            link(g.memset(causal[:, :], 0.0))
            for k0 in (0, 2 * P):
                g.affine_select(out=causal[:, k0:k0 + P], in_=causal[:, k0:k0 + P], compare_op=ALU.is_ge, fill=MASKED,
                                base=0, pattern=[[-1, P]], channel_multiplier=1).then_inc(causal_ready, 1)
            link(g.memset(neg8[:, :], 0.0))
            g.affine_select(out=neg8[:, :], in_=neg8[:, :], compare_op=ALU.not_equal, fill=-math.sqrt(HD), base=0,
                            pattern=[[-1, HEADS]], channel_multiplier=1).then_inc(neg8_ready, 1)
            g.iota(iota[:, :, :], pattern=[[0, 2], [1, SLOTS]], base=0, channel_multiplier=0,
                   allow_small_or_imprecise_dtypes=True).then_inc(iota_ready, 1)
            g.wait_ge(ylru_ready, 1)
            g.dma_start(gffn_b, g_ffn.rearrange("(a n) -> a n", a=1).broadcast_to([P, D])).then_inc(late_loaded, 16)
            g.dma_start(gfin_b, g_final.rearrange("(a n) -> a n", a=1).broadcast_to([P, D])).then_inc(late_loaded, 16)
            g.dma_start(bdn, b_down[:, :]).then_inc(late_loaded, 16)
            g.wait_ge(s_psum, HEADS)
            g.dma_start(bgu, b_gate_up[:, :]).then_inc(late_loaded, 16)
            g.wait_ge(chunk_done, C_WL + 4)
            g.memset(ones, 1.0).then_inc(ones_ready, 1)
            g.wait_ge(ones_ready, 1)
            g.affine_select(out=tri, in_=ones, compare_op=ALU.is_gt, fill=0.0, base=0,
                            pattern=[[1, P]], channel_multiplier=-1).then_inc(tri_ready, 1)

        @block.scalar
        def _(act):
            for src, r0 in ((g_mix, 0), (conv_b, 40), (b_rg, 48), (b_ig, 56), (lru_lambda, 64)):
                act.dma_start(rows[r0:r0 + KT, :], src.rearrange("(j p) -> j p", p=P)).then_inc(rows_loaded, 16)
            act.dma_start(rows[8:40, :], conv_w.rearrange("w (j p) -> (w j) p", p=P)).then_inc(rows_loaded, 16)
            act.dma_start(wf[:, :, :], w_in[:, F_COL:F_COL + HEADS].rearrange("(k p) n -> p k n", p=P)).then_inc(small_loaded, 16)
            act.dma_start(bf[:, :], b_f.rearrange("(h a) -> h a", a=1)).then_inc(small_loaded, 16)
            act.dma_start(wr[:, :, :], w_router.rearrange("(k p) n -> p k n", p=P)).then_inc(small_loaded, 16)
            act.dma_start(brt[:, :], b_router.rearrange("(a n) -> a n", a=1).broadcast_to([P, N_EXP])).then_inc(small_loaded, 16)
            steps = [0]

            def link(ins):
                steps[0] += 1
                ins.then_inc(act_step, 1)
                act.wait_ge(act_step, steps[0])

            act.wait_ge(x_loaded, 16)
            for t in range(TT):
                act.activation(lru_pad[:, 4 * t:4 * t + 4, 0:S], x_sb[:, t, :].rearrange("p (a b) -> p a b", a=4), ACT.Square,
                               accum_out=stat[:, t:t + 1]).then_inc(sumsq_ready, 1)
            act.wait_ge(sumsq_ready, TT)
            act.wait_ge(eps_ready, 1)
            act.activation(stat[:, 2:4], stat[:, 0:2], ACT.Sqrt, scale=1.0 / D, bias=epsc[:, 0:1]).then_inc(rms_ready, 1)

            def evac(c):
                g, j = c // 4 * 4, c % 4
                act.wait_ge(chunk_done, c + 1)
                src = pj[c % 2][:, :].rearrange("p (a s) -> p a s", a=2)
                if g == C_V:
                    dst = V[:, :, j * CC:(j + 1) * CC]
                elif g == C_LRU:
                    dst = lru_pad[:, 2 * j:2 * j + 2, CONV - 1:]
                else:
                    dst = {C_K: K, C_Q: Q, C_LG: LG, C_GL: GL, C_GF: GF}[g][:, 2 * j:2 * j + 2, :]
                act.activation(dst, src, ACT.Identity).then_inc(act_evac, 1)

            for c in range(4):
                evac(c)
            act.wait_ge(f_psum, 1)
            act.wait_ge(small_loaded, 64)
            link(act.activation(fz[:, 0, :], ga[0:HEADS, 0:S], ACT.Identity, bias=bf[:, 0:1]))
            link(act.activation(fz[:, 1, :], fz[:, 0, :], ACT.Abs))
            act.activation(fz[:, 2, :], fz[:, 1, :], ACT.Exp, scale=-1.0).then_inc(f_exp, 1)
            act.wait_ge(lam_abs, 1)
            act.activation(lam[:, 1, :], lam[:, 0, :], ACT.Exp, scale=-1.0).then_inc(lam_exp, 1)
            for c in range(4, 8):
                evac(c)
            for j in range(KT):
                evac(8 + j)
                act.wait_ge(gates_psum, j + 1)
                b = (ga, gb)[j % 2]
                act.activation(R[:, j, :], b[:, 0:S], ACT.Sigmoid, bias=vec[:, 48 + j:49 + j]).then_inc(ri_ready, 1)
                act.activation(I[:, j, :], b[:, S:2 * S], ACT.Sigmoid, bias=vec[:, 56 + j:57 + j]).then_inc(ri_ready, 1)
            act.wait_ge(loga_ready, KT)
            act.activation(mult, R[:, :, :], ACT.Tanh).then_inc(tanh_ready, 1)
            act.wait_ge(tanh_ready, 1)
            act.activation(R[:, :, :], R[:, :, :], ACT.Exp).then_inc(a_ready, 1)
            act.wait_ge(mult2_ready, 1)
            act.activation(mult, mult, ACT.Sqrt).then_inc(mult_ready, 1)

            for s in range(HEADS + 2):
                if s < HEADS:
                    act.wait_ge(logits_ready, s + 1)
                    for q, (lo, hi) in enumerate(((0, P), (P, 3 * P))):
                        n = 2 * (s % 2) + q
                        act.activation(L[:, s % 2, lo:hi], L[:, s % 2, lo:hi], ACT.Exp, scale=1 / math.sqrt(HD),
                                       bias=stat[:, 8 + n:9 + n], accum_out=stat[:, 12 + n:13 + n]).then_inc(exp_ready, 1)
                if s < 12:
                    evac(16 + s)
                if s % 2 == 0 and s >= 4:
                    j = s // 2 - 2
                    act.wait_ge(o_psum, 2 * j + 2)
                    act.activation(Q[:, j, :], ob[j % 2][:, 0:S], ACT.Identity).then_inc(o_evac, 1)
                if s == 7:
                    act.wait_ge(act_evac, C_GL + 4)
                    act.activation(LG[:, :, :], LG[:, :, :], ACT.Gelu_apprx_tanh).then_inc(gelu_ready, 1)
                    act.activation(GL[:, :, :], GL[:, :, :], ACT.Sigmoid).then_inc(gl_ready, 1)
            act.wait_ge(o_psum, HEADS)
            act.activation(Q[:, KT - 1, :], ob[1][:, 0:S], ACT.Identity).then_inc(o_evac, 1)
            act.wait_ge(act_evac, C_GF + 4)
            act.activation(GF[:, :, :], GF[:, :, :], ACT.Sigmoid).then_inc(gf_ready, 1)

            act.wait_ge(dve_evac, MIX_CHUNKS - C_WL)
            for t in range(TT):
                act.activation(flat(GL)[:, 0:D], x_sb[:, t, :], ACT.Square, accum_out=stat[:, 20 + t:21 + t]).then_inc(sumsq2, 1)
                act.wait_ge(sumsq2, t + 1)
            act.activation(stat[:, 22:24], stat[:, 20:22], ACT.Sqrt, scale=1.0 / D, bias=epsc[:, 0:1]).then_inc(rms2, 1)
            for j in (0, 2):
                act.wait_ge(h2T_psum, j + 1)
                act.activation(h2T[:, 2 * j:2 * j + 2, :].rearrange("p a b -> p (a b)"), acc[j // 2][j % 2][:, :],
                               ACT.Identity).then_inc(h2T_act, 1)
            for t in range(TT):
                act.wait_ge(neg_top, 1)
                act.activation(expw[:, t, :], lg[:, t, TOP_K:], ACT.Exp, bias=stat[:, 30 + t:31 + t]).then_inc(exp_top, 1)
            act.wait_ge(combT_psum, 1)
            act.activation(combT, gb[0:N_EXP, 0:S], ACT.Identity).then_inc(combT_ready, 1)

            def expert_round(b0, n0, t0):
                def hg_copy(b):
                    act.wait_ge(gathered, b + 1)
                    act.activation(hg[:, 0:KT // 2, :, :], ga[:, :].rearrange("p (k i s) -> p k i s", i=2, s=SLOTS),
                                   ACT.Identity).then_inc(hg_ready, 1)

                def sigmoid_of(n):
                    act.wait_ge(gate_ready, n + 1)
                    act.activation(sig, gate, ACT.Sigmoid, scale=ALPHA).then_inc(sig_ready, 1)

                def moves_of(n):
                    act.wait_ge(act_transposed, n + 1)
                    act.activation(actT, ga[:, :].rearrange("p (j h s) -> p j h s", h=2, s=SLOTS), ACT.Identity).then_inc(actT_ready, 1)
                    act.wait_ge(chunk_done, n * EXP_CHUNKS + MIX_CHUNKS + EXP_CHUNKS)
                    act.activation(Y, gb[:, :], ACT.Identity).then_inc(y_ready, 1)

                hg_copy(b0)
                with act.Fori(0, PAIRS) as p:
                    n = p * 2 + n0
                    sigmoid_of(n)
                    act.wait_ge(selw_transposed, p + t0 + 1)
                    act.activation(selWT, gb[:, :].rearrange("p (i n) -> p i n", i=2), ACT.Identity).then_inc(selwt_ready, 1)
                    moves_of(n)
                    sigmoid_of(n + 1)
                    hg_copy(p + b0 + 1)
                    moves_of(n + 1)

            expert_round(0, 0, 0)
            act.wait_ge(flag_ready, 1)
            over = act.value_load(flag_i[0:1, 0:1], min_val=0, max_val=1)
            with act.If(over > 0):
                with act.Fori(1, ROUNDS) as r:
                    expert_round(r * (PAIRS + 1), r * N_EXP, r * PAIRS)
            act.end_ifs()

            for t in range(TT):
                act.wait_ge(y_summed, 2 * t + 2)
                act.activation(flat(GL)[:, 0:D], yo[:, t, :], ACT.Square, accum_out=stat[:, 40 + t:41 + t]).then_inc(sumsq3, 1)
                act.wait_ge(sumsq3, t + 1)
                act.activation(stat[:, 42 + t:43 + t], stat[:, 40 + t:41 + t], ACT.Sqrt, scale=1.0 / D,
                               bias=epsc[:, 0:1]).then_inc(rms3, 1)

        @block.vector
        def _(dve):
            v = nc.vector
            steps = [0]

            def link(ins):
                steps[0] += 1
                ins.then_inc(dve_step, 1)
                dve.wait_ge(dve_step, steps[0])

            v.memset(epsc[:, :], RMS_EPS).then_inc(eps_ready, 1)
            dve.wait_ge(rms_ready, 1)
            link(v.reciprocal(stat[:, 4:6], stat[:, 2:4]))
            for t in range(TT):
                v.tensor_scalar(xs[:, t, :], x_sb[:, t, :], stat[:, 4 + t:5 + t], None, ALU.mult).then_inc(xs_ready, 1)
            v.memset(lru_pad[:, :, 0:CONV - 1], 0.0).then_inc(pad_ready, 1)
            dve.wait_ge(vec_psum, 1)
            v.tensor_copy(vec[:, :], ga[:, 0:72]).then_inc(vec_ready, 1)
            dve.wait_ge(vec_ready, 1)
            for j in range(KT):
                dve.wait_ge(hT_psum, j // 2 + 1)
                v.tensor_scalar(hT[:, j, :], (ps[0], ps[1], pt, po)[j // 2][:, S * (j % 2):S * (j % 2) + S],
                                vec[:, j:j + 1], None, ALU.mult).then_inc(hT_ready, 1)
            v.scalar_tensor_tensor(lam[:, 0, :], vec[:, 64:72], -1.0, vec[:, 64:72], ALU.mult, ALU.max).then_inc(lam_abs, 1)
            dve.wait_ge(pad_ready, 1)
            for j in range(KT):
                dve.wait_ge(act_evac, C_LRU + j // 2 + 1)
                link(v.tensor_scalar(XC[:, j, :], lru_pad[:, j, 0:S], vec[:, 8 + j:9 + j], vec[:, 40 + j:41 + j],
                                     ALU.mult, ALU.add))
                for i in range(1, CONV):
                    ins = v.scalar_tensor_tensor(XC[:, j, :], lru_pad[:, j, i:i + S], vec[:, 8 + i * KT + j:9 + i * KT + j],
                                                 XC[:, j, :], ALU.mult, ALU.add)
                    if i < CONV - 1:
                        link(ins)
                    else:
                        ins.then_inc(conv_ready, 1)

            def half_log1p(e, y, w, q):
                link(v.tensor_scalar(w, e, 2.0, None, ALU.add))
                link(v.reciprocal(w, w))
                link(v.tensor_tensor(y, e, w, ALU.mult))
                link(v.tensor_tensor(w, y, y, ALU.mult))
                link(v.tensor_scalar(q, w, 1.0 / 15.0, None, ALU.mult))
                for k in (13, 11, 9, 7, 5, 3):
                    link(v.scalar_tensor_tensor(q, q, 1.0 / k, w, ALU.add, ALU.mult))
                link(v.scalar_tensor_tensor(q, q, 1.0, y, ALU.add, ALU.mult))

            dve.wait_ge(lam_exp, 1)
            half_log1p(lam[:, 1, :], lam[:, 2, :], lam[:, 3, :], lam[:, 4, :])
            link(v.tensor_scalar(lam[:, 2, :], vec[:, 64:72], 0.0, LRU_C, ALU.min, ALU.mult))
            link(v.scalar_tensor_tensor(lam[:, 0, :], lam[:, 4, :], -2.0 * LRU_C, lam[:, 2, :], ALU.mult, ALU.add))
            dve.wait_ge(f_exp, 1)
            half_log1p(fz[:, 2, :], fz[:, 3, :], fz[:, 4, :], fz[:, 5, :])
            link(v.tensor_scalar(fz[:, 3, :], fz[:, 0, :], 0.0, None, ALU.min))
            link(v.scalar_tensor_tensor(fz[:, 4, :], fz[:, 5, :], -2.0, fz[:, 3, :], ALU.mult, ALU.add))
            link(v.memset(fz[:, 6, :], 1.0))
            v.tensor_tensor_scan(cumf[:, :], fz[:, 6, :], fz[:, 4, :], 0.0, ALU.mult, ALU.add).then_inc(cum_ready, 1)
            for j in range(KT):
                dve.wait_ge(ri_ready, 2 * j + 1)
                v.tensor_scalar(R[:, j, :], R[:, j, :], lam[:, 0, j:j + 1], None, ALU.mult).then_inc(loga_ready, 1)
            dve.wait_ge(cum_ready, 1)
            dve.wait_ge(tanh_ready, 1)
            link(v.tensor_scalar(one_t, mult, -1.0, 1.0, ALU.mult, ALU.add))
            link(v.reciprocal(one_t, one_t))
            v.scalar_tensor_tensor(mult, mult, -2.0, one_t, ALU.mult, ALU.mult).then_inc(mult2_ready, 1)
            dve.wait_ge(ri_ready, 2 * KT)
            dve.wait_ge(conv_ready, KT)
            link(v.tensor_tensor(I[:, :, :], I[:, :, :], XC[:, :, :], ALU.mult))

            for s in range(HEADS + 2):
                if 1 <= s <= HEADS:
                    b = (s - 1) % 2
                    dve.wait_ge(exp_ready, 2 * s)
                    link(v.reciprocal(stat[:, 16 + 2 * b:18 + 2 * b], stat[:, 12 + 2 * b:14 + 2 * b]))
                    for q, (lo, hi) in enumerate(((0, P), (P, 3 * P))):
                        v.tensor_scalar(L[:, b, lo:hi], L[:, b, lo:hi], stat[:, 16 + 2 * b + q:17 + 2 * b + q], None,
                                        ALU.mult).then_inc(p_ready, 1)
                if s >= 2:
                    dve.wait_ge(pt_psum, s - 1)
                    if s >= 4:
                        dve.wait_ge(o_psum, s - 3)
                    v.tensor_copy(PT[:, s % 2, :], pt[:, 0:3 * P]).then_inc(pt_ready, 1)
                if s < HEADS:
                    if s == 0:
                        dve.wait_ge(causal_ready, 2)
                    dve.wait_ge(s_psum, s + 1)
                    link(v.tensor_tensor(L[:, s % 2, :], ps[s % 2][:, 0:3 * P], causal[:, :], ALU.add))
                    n = 2 * (s % 2)
                    link(v.reduce_max(stat[:, 24:25], L[:, s % 2, 0:P], AX.X))
                    link(v.reduce_max(stat[:, 25:26], L[:, s % 2, P:3 * P], AX.X))
                    v.tensor_scalar(stat[:, 8 + n:10 + n], stat[:, 24:26], -1.0 / math.sqrt(HD), None,
                                    ALU.mult).then_inc(logits_ready, 1)
                    dve.wait_ge(logits_ready, s + 1)
                if s == 0:
                    dve.wait_ge(mult_ready, 1)
                    link(v.tensor_tensor(I[:, :, :], I[:, :, :], mult, ALU.mult))
                if 1 <= s <= KT:
                    dve.wait_ge(a_ready, 1)
                    link(v.tensor_tensor_scan(XC[:, s - 1, :], R[:, s - 1, :], I[:, s - 1, :], 0.0, ALU.mult, ALU.add))
                if s == KT + 1:
                    dve.wait_ge(gelu_ready, 1)
                    v.tensor_tensor(XC[:, :, :], XC[:, :, :], LG[:, :, :], ALU.mult).then_inc(ylru_ready, 1)
                if 12 <= s < HEADS:
                    c = s - 12
                    dve.wait_ge(gl_ready, 1)
                    dve.wait_ge(chunk_done, C_WL + c + 1)
                    v.tensor_tensor(mg[:, 2 * c:2 * c + 2, :], pj[c % 2][:, :].rearrange("p (a s) -> p a s", a=2),
                                    GL[:, 2 * c:2 * c + 2, :], ALU.mult).then_inc(dve_evac, 1)
            for c in range(4):
                dve.wait_ge(gf_ready, 1)
                dve.wait_ge(chunk_done, C_WF + c + 1)
                v.tensor_tensor(tmp, pj[c % 2][:, :].rearrange("p (a s) -> p a s", a=2),
                                GF[:, 2 * c:2 * c + 2, :], ALU.mult).then_inc(dve_evac, 1)
                dve.wait_ge(dve_evac, 4 + c + 1)
                v.tensor_tensor(mg[:, 2 * c:2 * c + 2, :], mg[:, 2 * c:2 * c + 2, :], tmp, ALU.add).then_inc(merged_ready, 1)
                dve.wait_ge(merged_ready, c + 1)
            for c in range(4):
                dve.wait_ge(chunk_done, C_WO + c + 1)
                v.tensor_tensor(x_sb[:, :, c * CC:(c + 1) * CC], x_sb[:, :, c * CC:(c + 1) * CC],
                                pj[c % 2][:, :].rearrange("p (a s) -> p a s", a=2), ALU.add).then_inc(dve_evac, 1)

            dve.wait_ge(rms2, 1)
            link(v.reciprocal(stat[:, 26:28], stat[:, 22:24]))
            dve.wait_ge(late_loaded, 64)
            for t in range(TT):
                v.scalar_tensor_tensor(h2[:, t, :], x_sb[:, t, :], stat[:, 26 + t:27 + t], gffn_b, ALU.mult,
                                       ALU.mult).then_inc(h2_ready, 1)
            for j in (1, 3):
                dve.wait_ge(h2T_psum, j + 1)
                v.tensor_copy(h2T[:, 2 * j:2 * j + 2, :].rearrange("p a b -> p (a b)"), acc[j // 2][j % 2][:, :]).then_inc(h2T_dve, 1)

            dve.wait_ge(chunk_done, C_WL + 4)
            link(v.memset(lg[:, :, 0:TOP_K], BIG))
            link(v.memset(pos[:, :, :], -1.0))
            dve.wait_ge(router_psum, 1)
            link(v.tensor_tensor(lg[:, :, TOP_K:], ga[:, 0:TT * N_EXP].rearrange("p (t e) -> p t e", t=TT),
                                 brt[:, :].unsqueeze(1).broadcast_to([P, TT, N_EXP]), ALU.add))
            for t in range(TT):
                link(v.max(top8[:, t, :], lg[:, t, :]))
            v.tensor_scalar(stat[:, 30:32], top8[:, :, TOP_K], -1.0, None, ALU.mult).then_inc(neg_top, 1)
            for t in range(TT):
                link(v.match_replace(rep[:, t, :], top8[:, t, :], lg[:, t, :], -BIG))
            v.tensor_tensor(msk, rep[:, :, TOP_K:], lg[:, :, TOP_K:], ALU.not_equal).then_inc(mask_ready, 1)
            dve.wait_ge(mask_ready, 1)
            dve.wait_ge(exp_top, TT)
            link(v.tensor_tensor(expw, expw, msk, ALU.mult))
            link(v.reduce_sum(stat[:, 32:34], expw, AX.X))
            link(v.reciprocal(stat[:, 34:36], stat[:, 32:34]))
            link(v.memset(comb[:, :, N_EXP:], 0.0))
            v.tensor_tensor(comb[:, :, 0:N_EXP], expw, stat[:, 34:36].unsqueeze(2).broadcast_to([P, TT, N_EXP]),
                            ALU.mult).then_inc(comb_ready, 1)
            dve.wait_ge(comb_ready, 1)
            dve.wait_ge(pos_psum, 1)
            link(v.scalar_tensor_tensor(pos[:, :, 0:N_EXP], ga[:, 256:256 + TT * N_EXP].rearrange("p (t e) -> p t e", t=TT),
                                        1.0, msk, ALU.add, ALU.mult))
            link(v.tensor_scalar(pos[:, :, 0:N_EXP], pos[:, :, 0:N_EXP], -1.0, None, ALU.add))

            def build_sel(e):
                v.tensor_tensor(sel, iota[:, :, :].rearrange("p a s -> p (a s)").unsqueeze(1).unsqueeze(1).broadcast_to([P, TT, 2, P])
                                , pos[:, :, bass.ds(e, 2)].unsqueeze(3).broadcast_to([P, TT, 2, P]),
                                ALU.is_equal).then_inc(sel_ready, 1)

            def weigh_sel(e):
                v.tensor_tensor(selW, sel, comb[:, :, bass.ds(e, 2)].unsqueeze(3).broadcast_to([P, TT, 2, P]),
                                ALU.mult).then_inc(sel_ready, 1)

            def build_onehot(e):
                v.tensor_copy(onehot, ident[0:N_EXP, bass.ds(e, 2)].unsqueeze(2).broadcast_to([N_EXP, 2, SLOTS])).then_inc(onehot_ready, 1)

            dve.wait_ge(iota_ready, 1)

            def expert_round(b0, n0, t0):
                def glu_of(n):
                    c0 = n * 2
                    dve.wait_ge(chunk_done, n * EXP_CHUNKS + MIX_CHUNKS + GU_CHUNKS)
                    v.tensor_scalar(gate, pj[0][:, :], LIMIT, None, ALU.min).then_inc(gate_ready, 1)
                    v.tensor_scalar(up, pj[1][:, :], LIMIT, -LIMIT, ALU.min, ALU.max).then_inc(moe_step, 1)
                    dve.wait_ge(gate_ready, n + 1)
                    dve.wait_ge(sig_ready, n + 1)
                    v.tensor_tensor(glu, gate, sig, ALU.mult).then_inc(moe_step, 1)
                    dve.wait_ge(moe_step, c0 + 2)
                    v.scalar_tensor_tensor(prod, up, 1.0, glu, ALU.add, ALU.mult).then_inc(act_ready, 1)

                def hg_copy(b):
                    dve.wait_ge(gathered, b + 1)
                    v.tensor_copy(hg[:, KT // 2:, :, :], gb[:, :].rearrange("p (k i s) -> p k i s", i=2, s=SLOTS)).then_inc(hg_ready, 1)

                build_sel(0)
                build_onehot(0)
                dve.wait_ge(sel_ready, b0 * 2 + 1)
                weigh_sel(0)
                hg_copy(b0)
                with dve.Fori(0, PAIRS) as p:
                    n, t, e = p * 2 + n0, p + t0, p * 2 + 2
                    glu_of(n)
                    dve.wait_ge(gathered, p + b0 + 1)
                    build_sel(e)
                    dve.wait_ge(selw_transposed, t + 1)
                    dve.wait_ge(sel_ready, (p + b0) * 2 + 3)
                    weigh_sel(e)
                    glu_of(n + 1)
                    build_onehot(e)
                    hg_copy(p + b0 + 1)

            v.tensor_reduce(stat[:, 36:37], pos[:, :, :], AX.XY, ALU.max).then_inc(maxp_ready, 1)
            dve.wait_ge(maxT_psum, 1)
            link(v.reduce_max(flag[0:1, 0:1], ga[0:1, 384:512], AX.X))
            link(v.tensor_scalar(flag[0:1, 1:2], flag[0:1, 0:1], float(SLOTS) - 0.5, None, ALU.is_gt))
            v.tensor_copy(flag_i[0:1, 0:1], flag[0:1, 1:2]).then_inc(flag_ready, 1)

            expert_round(0, 0, 0)
            dve.wait_ge(scattered, N_EXP)
            dve.wait_ge(flag_ready, 1)
            over = dve.value_load(flag_i[0:1, 0:1], min_val=0, max_val=1)
            with dve.If(over > 0):
                with dve.Fori(1, ROUNDS) as r:
                    dve.wait_ge(gathered, r * (PAIRS + 1))
                    v.tensor_scalar(pos[:, :, 0:N_EXP], pos[:, :, 0:N_EXP], -float(SLOTS), None,
                                    ALU.add).then_inc(moe_round, 1)
                    dve.wait_ge(moe_round, r)
                    expert_round(r * (PAIRS + 1), r * N_EXP, r * PAIRS)
                    dve.wait_ge(scattered, (r + 1) * N_EXP)
            dve.end_ifs()

            for t in range(TT):
                for h in range(2):
                    v.tensor_tensor(yo[:, t, h * 512:(h + 1) * 512], x_sb[:, t, h * 512:(h + 1) * 512], acc[t][h][:, :],
                                    ALU.add).then_inc(y_summed, 1)
            for t in range(TT):
                dve.wait_ge(rms3, t + 1)
                link(v.reciprocal(stat[:, 44 + t:45 + t], stat[:, 42 + t:43 + t]))
                dve.wait_ge(y_summed, 2 * t + 2)
                v.scalar_tensor_tensor(yo[:, t, :], yo[:, t, :], stat[:, 44 + t:45 + t], gfin_b, ALU.mult,
                                       ALU.mult).then_inc(final_ready, 1)

        @block.tensor
        def _(pe):
            mm = nc.tensor.matmul

            pe.wait_ge(ident_ready, 1)
            pe.wait_ge(rows_loaded, 96)
            nc.tensor.transpose(ga[:, 0:72], rows[:, :], ident[0:72, 0:72]).then_inc(vec_psum, 1)
            pe.wait_ge(xs_ready, TT)
            for j in range(KT):
                for t in range(TT):
                    c0 = S * (j % 2) + t * P
                    last = nc.tensor.transpose((ps[0], ps[1], pt, po)[j // 2][:, c0:c0 + P], xs[:, t, j * P:(j + 1) * P], ident[:, :])
                if j % 2:
                    last.then_inc(hT_psum, 1)
            pe.wait_ge(hT_ready, KT)
            pe.wait_ge(vec_ready, 1)
            pe.wait_ge(small_loaded, 64)
            for k in range(KT):
                last = mm(ga[0:HEADS, 0:S], wf[:, k, :], hT[:, k, :], start=(k == 0), stop=(k == KT - 1))
            last.then_inc(f_psum, 1)

            def free_pj(c):
                if c - 2 >= C_WL:
                    pe.wait_ge(dve_evac, c - 1 - C_WL)
                elif c >= 2:
                    pe.wait_ge(act_evac, c - 1)

            def chunk(c):
                w = ring[:, c % RING, :].rearrange("p (k n) -> p k n", k=KT)
                g = c // 4 * 4
                pe.wait_ge(loaded[c % RING], 16 * (c // RING + 1))
                free_pj(c)
                for a in range(2):
                    for k in range(KT):
                        if g == C_V:
                            lhs, rhs = hT[:, k, a * P:(a + 1) * P], w[:, k, :]
                        elif g == C_WO:
                            lhs, rhs = mg[:, k, a * P:(a + 1) * P], w[:, k, :]
                        else:
                            lhs, rhs = w[:, k, a * P:(a + 1) * P], {C_WL: XC, C_WF: Q}.get(g, hT)[:, k, :]
                        last = mm(pj[c % 2][:, a * S:(a + 1) * S], lhs, rhs, start=(k == 0), stop=(k == KT - 1))
                last.then_inc(chunk_done, 1)

            for c in range(8):
                chunk(c)
            for j in range(KT):
                chunk(8 + j)
                if j == 0:
                    pe.wait_ge(gatew_loaded, 64)
                pe.wait_ge(conv_ready, j + 1)
                if j >= 2:
                    pe.wait_ge(ri_ready, 2 * (j - 1))
                else:
                    pe.wait_ge(f_exp, 1)
                b = (ga, gb)[j % 2]
                mm(b[:, 0:S], wrg_bd[:, j, :], XC[:, j, :], start=True, stop=True)
                mm(b[:, S:2 * S], wig_bd[:, j, :], XC[:, j, :], start=True, stop=True).then_inc(gates_psum, 1)

            for s in range(HEADS + 2):
                if s < HEADS:
                    if s == 0:
                        pe.wait_ge(act_evac, C_V + 4)
                        pe.wait_ge(cum_ready, 1)
                        pe.wait_ge(neg8_ready, 1)
                    if s >= 2:
                        pe.wait_ge(logits_ready, s - 1)
                    j, r0 = s // 2, HD * (s % 2)
                    for q, (c0, n) in enumerate(((0, P), (P, 2 * P))):
                        mm(ps[s % 2][:, c0:c0 + n], Q[r0:r0 + HD, j, q * P:(q + 1) * P], K[r0:r0 + HD, j, 0:n],
                           start=True, stop=False)
                        last = mm(ps[s % 2][:, c0:c0 + n], neg8[:, s:s + 1].broadcast_to([HEADS, P]), cumf[:, 0:n],
                                  start=False, stop=True)
                    last.then_inc(s_psum, 1)
                    if 16 + s == C_WL:
                        pe.wait_ge(ylru_ready, 1)
                    chunk(16 + s)
                if 1 <= s <= HEADS:
                    pe.wait_ge(p_ready, 2 * s)
                    if s >= 2:
                        pe.wait_ge(pt_ready, s - 1)
                    for b in range(3):
                        last = nc.tensor.transpose(pt[:, b * P:(b + 1) * P], L[:, (s - 1) % 2, b * P:(b + 1) * P], ident[:, :])
                    last.then_inc(pt_psum, 1)
                if s >= 2:
                    h = s - 2
                    j, r0 = h // 2, HD * (h % 2)
                    pe.wait_ge(pt_ready, h + 1)
                    if j >= 2:
                        pe.wait_ge(o_evac, j - 1)
                    elif j == 1:
                        pe.wait_ge(ri_ready, 2 * KT)
                    o = ob[j % 2][r0:r0 + HD, 0:S]
                    mm(o[:, 0:P], V[:, 0, h * HD:(h + 1) * HD], PT[:, h % 2, 0:P], start=True, stop=True)
                    mm(o[:, P:2 * P], V[:, 0, h * HD:(h + 1) * HD], PT[:, h % 2, P:2 * P], start=True, stop=False)
                    mm(o[:, P:2 * P], V[:, 1, h * HD:(h + 1) * HD], PT[:, h % 2, 2 * P:3 * P], start=False,
                       stop=True).then_inc(o_psum, 1)
            pe.wait_ge(o_evac, KT)
            for c in range(C_WF, C_WF + 4):
                chunk(c)
            pe.wait_ge(merged_ready, 4)
            for c in range(C_WO, C_WO + 4):
                chunk(c)

            pe.wait_ge(h2_ready, TT)
            for j in range(KT):
                for t in range(TT):
                    c0 = S * (j % 2) + t * P
                    last = nc.tensor.transpose(acc[j // 4][j // 2 % 2][:, c0:c0 + P], h2[:, t, j * P:(j + 1) * P], ident[:, :])
                if j % 2:
                    last.then_inc(h2T_psum, 1)
            pe.wait_ge(h2T_act, 2)
            pe.wait_ge(h2T_dve, 2)
            for t in range(TT):
                for k in range(KT):
                    last = mm(ga[:, t * N_EXP:(t + 1) * N_EXP], h2T[:, k, t * P:(t + 1) * P], wr[:, k, :], start=(k == 0),
                              stop=(k == KT - 1))
            last.then_inc(router_psum, 1)
            pe.wait_ge(tri_ready, 1)
            pe.wait_ge(mask_ready, 1)
            mm(ga[:, 256:256 + N_EXP], tri, msk[:, 0, :], start=True, stop=True)
            mm(ga[:, 256 + N_EXP:256 + 2 * N_EXP], ones, msk[:, 0, :], start=True, stop=False)
            mm(ga[:, 256 + N_EXP:256 + 2 * N_EXP], tri, msk[:, 1, :], start=False, stop=True).then_inc(pos_psum, 1)
            pe.wait_ge(comb_ready, 1)
            pe.wait_ge(late_loaded, 64)
            for t in range(TT):
                last = nc.tensor.transpose(gb[0:N_EXP, t * P:(t + 1) * P], comb[:, t, 0:N_EXP], ident[:, :])
            last.then_inc(combT_psum, 1)
            pe.wait_ge(maxp_ready, 1)
            nc.tensor.transpose(ga[0:1, 384:512], stat[:, 36:37], ident[:, :]).then_inc(maxT_psum, 1)
            pe.wait_ge(combT_ready, 1)
            for t in range(TT):
                for h in range(2):
                    mm(acc[t][h][:, :], combT[:, t * P:(t + 1) * P], bdn[:, h * 512:(h + 1) * 512], start=True, stop=True,
                       skip_group_check=True)
            pe.wait_ge(flag_ready, 1)

            def expert_round(b0, n0, t0):
                def gather():
                    for k in range(KT):
                        for t in range(TT):
                            last = mm((ga, gb)[k // 4][:, k % 4 * P:(k % 4 + 1) * P], h2[:, t, k * P:(k + 1) * P],
                                      sel[:, t, :, 0:SLOTS], start=(t == 0), stop=(t == TT - 1))
                    last.then_inc(gathered, 1)

                def chunk_here(n, c):
                    slot = (EXP_SHIFT + c) % RING
                    pe.wait_ge(loaded[slot], n * 16 + 16 * (MIX_CHUNKS // RING + 1 + (EXP_SHIFT + c) // RING))
                    return slot

                def gate_up(n, i):
                    for q in range(4):
                        h = SLOTS * (q % 2)
                        mm(pj[q // 2][h:h + SLOTS, :], onehot[:, i, :], bgu[:, q * 512:(q + 1) * 512], start=True, stop=False)
                    for c in range(GU_CHUNKS):
                        slot = chunk_here(n, c)
                        for q in range(4):
                            h = SLOTS * (q % 2)
                            last = mm(pj[q // 2][h:h + SLOTS, :], hg[:, c, i, :], ring[:, slot, q * 512:(q + 1) * 512],
                                      start=False, stop=(c == GU_CHUNKS - 1))
                        last.then_inc(chunk_done, 1)

                def down(n):
                    pe.wait_ge(act_ready, n + 1)
                    for j in range(4):
                        last = nc.tensor.transpose(ga[:, j * P:(j + 1) * P], prod[:, j * P:(j + 1) * P], ident[:, :])
                    last.then_inc(act_transposed, 1)
                    pe.wait_ge(actT_ready, n + 1)
                    for c in range(DN_CHUNKS):
                        slot = chunk_here(n, GU_CHUNKS + c)
                        for a in range(2):
                            f = 2 * c + a
                            for q in range(2):
                                h = SLOTS * q
                                last = mm(gb[h:h + SLOTS, :], actT[:, f % 4, f // 4, :],
                                          ring[:, slot, a * D + q * 512:a * D + (q + 1) * 512], start=(f == 0), stop=(f == KT - 1))
                        last.then_inc(chunk_done, 1)

                def scatter(n, i):
                    pe.wait_ge(y_ready, n + 1)
                    for t in range(TT):
                        for q in range(2):
                            h = SLOTS * q
                            last = mm(acc[t][q][:, :], selWT[h:h + SLOTS, i, t * P:(t + 1) * P], Y[h:h + SLOTS, :],
                                      start=False, stop=True, skip_group_check=True)
                    last.then_inc(scattered, 1)

                pe.wait_ge(sel_ready, b0 * 2 + 1)
                pe.wait_ge(onehot_ready, b0 + 1)
                gather()
                with pe.Fori(0, PAIRS) as p:
                    n, b = p * 2 + n0, p + b0
                    pe.wait_ge(hg_ready, b * 2 + 2)
                    pe.wait_ge(onehot_ready, b + 1)
                    gate_up(n, 0)
                    pe.wait_ge(sel_ready, b * 2 + 2)
                    for i in range(2):
                        for t in range(TT):
                            last = nc.tensor.transpose(gb[:, (i * TT + t) * P:(i * TT + t + 1) * P], selW[:, t, i, :], ident[:, :])
                    last.then_inc(selw_transposed, 1)
                    pe.wait_ge(selwt_ready, p + t0 + 1)
                    down(n)
                    scatter(n, 0)
                    gate_up(n + 1, 1)
                    pe.wait_ge(sel_ready, b * 2 + 3)
                    gather()
                    pe.wait_ge(hg_ready, b * 2 + 4)
                    down(n + 1)
                    scatter(n + 1, 1)

            expert_round(0, 0, 0)
            over = pe.value_load(flag_i[0:1, 0:1], min_val=0, max_val=1)
            with pe.If(over > 0):
                with pe.Fori(1, ROUNDS) as r:
                    expert_round(r * (PAIRS + 1), r * N_EXP, r * PAIRS)
            pe.end_ifs()


_INS = ["x", "g_mix", "w_in", "conv_w", "conv_b", "w_rg", "b_rg", "w_ig", "b_ig", "lru_lambda", "b_f", "w_lru_out",
        "w_fox_out", "w_o", "g_ffn", "w_router", "b_router", "w_gate_up", "b_gate_up", "w_down", "b_down", "g_final"]


def kernel(**inputs):
    import concourse.bacc as bacc
    from concourse.bass_utils import run_bass_kernel_spmd

    nc = bacc.Bacc("TRN2", target_bir_lowering=False, num_devices=1)
    arrays, args = {}, []
    for name in _INS:
        a = np.ascontiguousarray(inputs[name])
        arrays[f"in_{name}"] = a
        args.append(nc.dram_tensor(f"in_{name}", a.shape, mybir.dt.from_np(a.dtype), kind="ExternalInput").ap())
    out = nc.dram_tensor("out_0", inputs["x"].shape, F32, kind="ExternalOutput").ap()
    hybrid_block(nc, *args, out)
    r = run_bass_kernel_spmd(nc, [arrays], core_ids=[0])
    return r.results[0]["out_0"]
```

```python
import math
from contextlib import ExitStack

import numpy as np
import concourse.bass as bass
from concourse import mybir

F32 = mybir.dt.float32
F32R = mybir.dt.float32r
I32 = mybir.dt.int32
ALU = mybir.AluOpType
ACT = mybir.ActivationFunctionType
AX = mybir.AxisListType

P = 128
S, D = 256, 1024
TT = S // P
KT = D // P
HEADS, HD = 16, 64
F_REST, F_ROWS = 96, 112
N_EXP, TOP_K, FF = 32, 4, 1024
CONV = 4
RMS_EPS = 1e-6
LRU_C = 8.0
LIMIT, ALPHA = 7.0, 1.702
MASKED = -1e30
BIG = 3.0e38

CC = 256
CHUNK = 2048
RING = 12
MIX_RING = 8
SLOTS = 64
ROUNDS = S // SLOTS
PAIRS = N_EXP // 2
GU_CHUNKS, DN_CHUNKS = KT, KT // 2
EXP_CHUNKS = GU_CHUNKS + DN_CHUNKS
assert EXP_CHUNKS == RING

C_LRU, C_K, C_Q, C_V, C_LG, C_GL, C_GF, C_WL, C_WF, C_WO = (4 * i for i in range(10))
MIX_CHUNKS = 40
W_IN_COL = {C_LRU: 0, C_K: 3072, C_Q: 2048, C_V: 4096, C_LG: 1024, C_GL: 5136, C_GF: 6160}
F_COL = 5120
assert MIX_CHUNKS % MIX_RING == 0
EXTRA = (0, 1, 2, 8, 9)
NVEC = 80
V_GMIX, V_CONVW, V_CONVB, V_BRG, V_BIG, V_LAM, V_GFFN = 0, 8, 40, 48, 56, 64, 72


def hybrid_block(nc, x, g_mix, w_in, conv_w, conv_b, w_rg, b_rg, w_ig, b_ig, lru_lambda, b_f,
                 w_lru_out, w_fox_out, w_o, g_ffn, w_router, b_router, w_gate_up, b_gate_up,
                 w_down, b_down, g_final, out):
    ctx = ExitStack()
    with ctx:
        def sb(name, shape, dt=F32):
            return ctx.enter_context(nc.sbuf_tensor(name, shape, dt))

        def bank(name):
            return ctx.enter_context(nc.psum_tensor(name, [P, 512], F32))

        def sem(name):
            return ctx.enter_context(nc.semaphore(name))

        def alias(name, shape, dt, at):
            return nc.alloc_sbuf_tensor_at(name, shape, dt, offset=at)

        BUF = 4 * CHUNK
        PADDED = 4 * KT * (S + CONV - 1)
        slab_bytes = RING * BUF + 11 * BUF + PADDED
        sb("slab", [P, slab_bytes // 4])
        where = [nc.sbuf_base - slab_bytes]

        def take(n=BUF):
            at = where[0]
            where[0] += n
            return at

        ring_at = take(RING * BUF)
        ring = alias("ring", [P, RING, CHUNK], F32, ring_at)
        w_hi = [alias(f"w_hi{i}", [P, KT, CC], F32R, ring_at + (MIX_RING + i) * BUF) for i in range(2)]
        w_lo = [alias(f"w_lo{i}", [P, KT, CC], F32R, ring_at + (MIX_RING + 2 + i) * BUF) for i in range(2)]
        x_sb = alias("x_sb", [P, TT, D], F32, take())
        hh_at, hl_at = take(), take()
        hT_hi = alias("hT_hi", [P, KT, S], F32R, hh_at)
        hT_lo = alias("hT_lo", [P, KT, S], F32R, hl_at)
        lp_at = take(PADDED)
        lru_pad = alias("lru_pad", [P, KT, S + CONV - 1], F32, lp_at)
        xc_at = take()
        XC = alias("XC", [P, KT, S], F32, xc_at)
        r_at, i_at = take(), take()
        R = alias("R", [P, KT, S], F32, r_at)
        I = alias("I", [P, KT, S], F32, i_at)
        y_hi = alias("y_hi", [P, KT, S], F32R, r_at)
        y_lo = alias("y_lo", [P, KT, S], F32R, i_at)
        lg_at = take()
        LG = alias("LG", [P, KT, S], F32, lg_at)
        q_at = take()
        Q = alias("Q", [P, KT, S], F32, q_at)
        k_at = take()
        K = alias("K", [P, KT, S], F32, k_at)
        v_at = take()
        V = alias("V", [P, TT, D], F32, v_at)
        gl_at = take()
        GL = alias("GL", [P, KT, S], F32, gl_at)
        GF = alias("GF", [P, KT, S], F32, lp_at)
        L = sb("L", [P, 2, 3 * P])
        PT = sb("PT", [P, 2, 3 * P])
        causal = sb("causal", [P, 3 * P])
        ident = sb("ident", [P, P])
        pick = sb("pick", [P, N_EXP + 2])
        rest_row = sb("rest_row", [P, 1])
        same_half = sb("same_half", [P, P])
        rows = sb("rows", [NVEC, P])
        vec = sb("vec", [P, NVEC])
        wr = sb("wr", [P, KT, N_EXP])
        neg8 = sb("neg8", [F_ROWS, HEADS])
        neg8_r = sb("neg8_r", [F_ROWS, HEADS], F32R)
        iota = sb("iota", [P, 2, SLOTS])
        stat = sb("stat", [P, 96])
        lam = sb("lam", [P, 5, KT])
        bf = sb("bf", [F_ROWS, 1])
        brt = sb("brt", [P, N_EXP])
        epsc = sb("epsc", [P, 1])
        flag = sb("flag", [1, 4])
        flag_i = sb("flag_i", [1, 1], I32)
        cumf_r = sb("cumf_r", [F_ROWS, S], F32R)

        def flat(t):
            return t[:, :, :].rearrange("p a b -> p (a b)")

        wrg_bd = flat(GL)[:, 0:1024].rearrange("p (j o) -> p j o", j=KT)
        wig_bd = flat(GL)[:, 1024:2048].rearrange("p (j o) -> p j o", j=KT)
        wf = flat(V)[:, 0:KT * F_ROWS].rearrange("p (k n) -> p k n", k=KT)
        fz = flat(LG)[0:F_ROWS, 0:2048].rearrange("p (n s) -> p n s", n=8)
        cumf = fz[:, 7, :]
        cumf_part = alias("cumf_part", [F_ROWS, S], F32R, lg_at + 5 * 4 * S)
        hT32 = XC
        mult = flat(lru_pad)[:, 0:2048].rearrange("p (j s) -> p j s", j=KT)
        xs = flat(K).rearrange("p (t d) -> p t d", t=TT)
        a_sq = flat(GL)[:, 0:2048].rearrange("p (j s) -> p j s", j=KT)
        mg = XC
        tmp = GL[:, 0:2, :]
        h2 = alias("h2", [P, TT, D], F32, hh_at)
        extra = {c: alias(f"extra{c}", [P, CHUNK], F32, at) for c, at in zip(EXTRA, (xc_at, lp_at, hl_at, r_at, q_at))}
        mo = alias("mo", [P, CHUNK], F32, i_at)
        yo = alias("yo", [P, TT, D], F32, r_at)
        h2T = Q
        bgu_raw = flat(K)[:, 0:1024]
        bgu = alias("bgu", [P, 1024], F32R, k_at)
        bgu_part = alias("bgu_part", [P, 1024], F32R, k_at + 4 * 1024)
        gffn_b = flat(LG)[:, 0:1024]
        bdn = flat(LG)[0:N_EXP, 1024:2048]
        gfin_b = extra[2][:, 0:D]
        gate = flat(V)[:, 0:512]
        sig = flat(V)[:, 512:1024]
        up = flat(V)[:, 1024:1536]
        glu = flat(V)[:, 1536:2048]
        prod = mo[:, 0:512]
        Y = mo[:, 512:1024]
        actT = mo[:, 1024:1536].rearrange("p (j h s) -> p j h s", h=2, s=SLOTS)
        hg = flat(GL)[:, 0:1024].rearrange("p (k i s) -> p k i s", k=KT, i=2)
        selWT = flat(GL)[:, 1024:1536].rearrange("p (i n) -> p i n", i=2)
        onehot = alias("onehot", [P, 2, P], F32R, gl_at + 4 * 1536)
        sel = flat(L)[:, 0:512].rearrange("p (t i s) -> p t i s", t=TT, i=2)
        combT = flat(L)[0:N_EXP, 512:768]
        selW = flat(PT)[:, 0:512].rearrange("p (t i s) -> p t i s", t=TT, i=2)
        EW = N_EXP + TOP_K
        lg = flat(V)[:, 0:TT * EW].rearrange("p (t e) -> p t e", t=TT)
        rep = flat(V)[:, 128:128 + TT * EW].rearrange("p (t e) -> p t e", t=TT)
        top8 = flat(V)[:, 208:224].rearrange("p (t e) -> p t e", t=TT)
        msk = flat(V)[:, 256:320].rearrange("p (t e) -> p t e", t=TT)
        expw = flat(V)[:, 320:384].rearrange("p (t e) -> p t e", t=TT)
        tri = flat(V)[:, 512:640]
        ones = flat(V)[:, 640:768]
        comb = flat(GL)[:, 1920:1920 + TT * EW].rearrange("p (t e) -> p t e", t=TT)
        pos = flat(GL)[:, 1792:1792 + TT * EW].rearrange("p (t e) -> p t e", t=TT)
        sq = [flat(V)[:, 1024:2048], flat(GL)[:, 0:1024]]

        pj = [bank("pj0"), bank("pj1")]
        ps = [bank("s0"), bank("s1")]
        pt, po = bank("pt"), bank("po")
        ga, gb = bank("ga"), bank("gb")
        ob = [po, ga]
        acc = [[ps[0], ps[1]], [pt, po]]

        loaded = [sem(f"slot{i}_loaded") for i in range(RING)]
        extra_loaded = {c: sem(f"extra{c}_loaded") for c in EXTRA}
        x_loaded = [sem(f"x{t}_loaded") for t in range(TT)]
        rows_loaded, gatew_loaded, small_loaded, late_loaded, gfin_loaded = (
            sem(n) for n in ("rows_loaded", "gatew_loaded", "small_loaded", "late_loaded", "gfin_loaded"))
        ident_ready, pick_ready, causal_ready, neg8_ready, iota_ready, f_zeroed, tri_ready, ones_ready, gatew_zeroed = (
            sem(n) for n in ("ident_ready", "pick_ready", "causal_ready", "neg8_ready", "iota_ready", "f_zeroed", "tri_ready", "ones_ready",
                             "gatew_zeroed"))
        gp_step, act_step, dve_step = sem("gp_step"), sem("act_step"), sem("dve_step")
        chunk_done = sem("chunk_done")
        hi_ready, lo_dve_ready, lo_pool_ready = sem("hi_ready"), sem("lo_dve_ready"), sem("lo_pool_ready")
        act_evac, dve_evac = sem("act_evac"), sem("dve_evac")
        hT32_ready, hT_hi_ready, hT_lo_ready = sem("hT32_ready"), sem("hT_hi_ready"), sem("hT_lo_ready")
        y_hi_ready, y_lo_ready, o_hi_ready, o_lo_ready, m_hi_ready, m_lo_ready = (
            sem(n) for n in ("y_hi_ready", "y_lo_ready", "o_hi_ready", "o_lo_ready", "m_hi_ready", "m_lo_ready"))
        eps_ready, sumsq_ready, rms_ready, xs_ready, vec_psum, vec_ready, hT_psum, wr_ready = (
            sem(n) for n in ("eps_ready", "sumsq_ready", "rms_ready", "xs_ready", "vec_psum", "vec_ready", "hT_psum",
                             "wr_ready"))
        pad_ready, conv_even, conv_ready, gates_psum, ri_ready, loga_ready, tanh_ready, a_ready, mult2_ready, mult_ready = (
            sem(n) for n in ("pad_ready", "conv_even", "conv_ready", "gates_psum", "ri_ready", "loga_ready", "tanh_ready", "a_ready",
                             "mult2_ready", "mult_ready"))
        lam_abs, lam_exp, gelu_ready, gl_ready, gf_ready, ylru_ready, scans_done, merged_ready = (
            sem(n) for n in ("lam_abs", "lam_exp", "gelu_ready", "gl_ready", "gf_ready", "ylru_ready", "scans_done", "merged_ready"))
        f_psum, f_exp, cum_ready, s_psum, logits_ready, exp_ready, p_ready, pt_psum, pt_ready, o_psum, o_evac = (
            sem(n) for n in ("f_psum", "f_exp", "cum_ready", "s_psum", "logits_ready", "exp_ready", "p_ready", "pt_psum",
                             "pt_ready", "o_psum", "o_evac"))
        sumsq2, sumsq2_ready, rms2, rs2_ready, h2_scaled, bgu_part_ready, bgu_split, rest_row_ready, h2T_psum, h2T_ready, router_psum, neg_top, exp_top, mask_ready, pos_psum = (
            sem(n) for n in ("sumsq2", "sumsq2_ready", "rms2", "rs2_ready", "h2_scaled", "bgu_part_ready", "bgu_split", "rest_row_ready", "h2T_psum", "h2T_ready", "router_psum", "neg_top",
                             "exp_top", "mask_ready", "pos_psum"))
        h2_ready = [sem(f"h2_ready{t}") for t in range(TT)]
        comb_ready, combT_psum, combT_ready, maxp_ready, maxT_psum, flag_ready = (
            sem(n) for n in ("comb_ready", "combT_psum", "combT_ready", "maxp_ready",
                             "maxT_psum", "flag_ready"))
        sel_ready, onehot_ready, gathered, hg_ready, gate_ready, sig_ready, act_ready = (
            sem(n) for n in ("sel_ready", "onehot_ready", "gathered", "hg_ready", "gate_ready", "sig_ready", "act_ready"))
        selw_transposed, selwt_ready, act_transposed, actT_ready, y_ready, scattered, moe_step = (
            sem(n) for n in ("selw_transposed", "selwt_ready", "act_transposed", "actT_ready", "y_ready",
                             "scattered", "moe_step"))
        moe_round = sem("moe_round")
        y_summed, sumsq3, sum3_ready, rms3, final_ready, out_stored = (
            sem(n) for n in ("y_summed", "sumsq3", "sum3_ready", "rms3", "final_ready", "out_stored"))

        block = ctx.enter_context(nc.Block())

        def mixer_chunk_src(c):
            g = c // 4 * 4
            if g in W_IN_COL:
                w, col = w_in, W_IN_COL[g] + (c - g) * CC
            else:
                w, col = {C_WL: w_lru_out, C_WF: w_fox_out, C_WO: w_o}[g], (c - g) * CC
            return w[:, col:col + CC].rearrange("(k p) n -> p k n", p=P)

        @block.sync
        def _(sp):
            for t in range(TT):
                sp.dma_start(x_sb[:, t, :], x[0, t * P:(t + 1) * P, :]).then_inc(x_loaded[t], 16)
            for src, r0 in ((g_mix, V_GMIX), (conv_b, V_CONVB), (b_rg, V_BRG), (b_ig, V_BIG), (lru_lambda, V_LAM), (g_ffn, V_GFFN)):
                sp.dma_start(rows[r0:r0 + KT, :], src.rearrange("(j p) -> j p", p=P)).then_inc(rows_loaded, 16)
            sp.dma_start(rows[8:40, :], conv_w.rearrange("w (j p) -> (w j) p", p=P)).then_inc(rows_loaded, 16)
            for c in range(MIX_CHUNKS):
                if c == 2:
                    sp.wait_ge(f_zeroed, 2)
                    for r0 in (0, F_REST):
                        sp.dma_start(wf[:, :, r0:r0 + HEADS], w_in[:, F_COL:F_COL + HEADS].rearrange("(k p) n -> p k n", p=P)).then_inc(small_loaded, 16)
                        sp.dma_start(bf[r0:r0 + HEADS, :], b_f.rearrange("(h a) -> h a", a=1)).then_inc(small_loaded, 16)
                    sp.dma_start(wr[:, :, :], w_router.rearrange("(k p) n -> p k n", p=P)).then_inc(small_loaded, 16)
                    sp.dma_start(brt[:, :], b_router.rearrange("(a n) -> a n", a=1).broadcast_to([P, N_EXP])).then_inc(small_loaded, 16)
                if c >= MIX_RING:
                    sp.wait_ge(lo_dve_ready, c - MIX_RING + 1)
                    sp.wait_ge(lo_pool_ready, c - MIX_RING + 1)
                sp.dma_start(ring[:, c % MIX_RING, :].rearrange("p (k n) -> p k n", k=KT),
                             mixer_chunk_src(c)).then_inc(loaded[c % MIX_RING], 16)

            def load_chunk(e, c, buf, loaded_sem):
                if c < GU_CHUNKS:
                    src = w_gate_up[bass.ds(e, 1), c * P:(c + 1) * P, :].rearrange("e p n -> p (e n)")
                else:
                    j = c - GU_CHUNKS
                    src = w_down[bass.ds(e, 1), 2 * j * P:2 * (j + 1) * P, :].rearrange("e (i p) n -> p (e i) n", p=P)
                    buf = buf.rearrange("p (i n) -> p i n", i=2)
                sp.dma_start(buf, src).then_inc(loaded_sem, 16)

            def ring_after_split(e, c):
                sp.wait_ge(lo_dve_ready, MIX_CHUNKS - MIX_RING + c + 1)
                sp.wait_ge(lo_pool_ready, MIX_CHUNKS - MIX_RING + c + 1)
                load_chunk(e, c, ring[:, c, :], loaded[c])

            def load_extra(c):
                load_chunk(0, c, extra[c][:, :], extra_loaded[c])

            for c in (0, 1, 2):
                ring_after_split(1, c)
            for c in (3, 4):
                ring_after_split(0, c)
            sp.wait_ge(chunk_done, C_WF + 4)
            load_extra(2)
            ring_after_split(0, 5)
            sp.wait_ge(m_lo_ready, 4)
            load_extra(0)
            load_extra(1)
            ring_after_split(0, 6)
            ring_after_split(0, 7)
            sp.wait_ge(chunk_done, MIX_CHUNKS - 1)
            load_chunk(0, 10, ring[:, 10, :], loaded[10])
            sp.wait_ge(chunk_done, MIX_CHUNKS)
            load_extra(8)
            load_chunk(0, 11, ring[:, 11, :], loaded[11])
            sp.wait_ge(router_psum, 1)
            load_extra(9)
            for c in (8, 9):
                load_chunk(1, c, ring[:, c, :], loaded[c])

            def load_expert(e, first, chunks=range(EXP_CHUNKS)):
                for c in chunks:
                    sp.wait_ge(chunk_done, first + (c - RING + 1))
                    load_chunk(e, c, ring[:, c, :], loaded[c])

            load_expert(1, EXP_CHUNKS + MIX_CHUNKS, [c for c in range(EXP_CHUNKS) if c not in EXTRA])
            with sp.Fori(2, N_EXP) as e:
                load_expert(e, e * EXP_CHUNKS + MIX_CHUNKS)
            sp.wait_ge(flag_ready, 1)
            over = sp.value_load(flag_i[0:1, 0:1], min_val=0, max_val=1)
            with sp.If(over > 0):
                with sp.Fori(1, ROUNDS) as r:
                    with sp.Fori(0, N_EXP) as e:
                        load_expert(e, r * (N_EXP * EXP_CHUNKS) + e * EXP_CHUNKS + MIX_CHUNKS)
            sp.end_ifs()
            for t in range(TT):
                sp.wait_ge(final_ready, t + 1)
                sp.dma_start(out[0, t * P:(t + 1) * P, :], yo[:, t, :]).then_inc(out_stored, 16)
            sp.wait_ge(out_stored, 16 * TT)

        @block.gpsimd
        def _(g):
            steps = [0]

            def link(ins):
                steps[0] += 1
                ins.then_inc(gp_step, 1)
                g.wait_ge(gp_step, steps[0])

            link(g.memset(ident[:, :], 0.0))
            g.affine_select(out=ident[:, :], in_=ident[:, :], compare_op=ALU.not_equal, fill=1.0, base=0,
                            pattern=[[-1, P]], channel_multiplier=1).then_inc(ident_ready, 1)
            g.memset(flat(GL), 0.0).then_inc(gatew_zeroed, 1)
            g.wait_ge(gatew_zeroed, 1)
            for w, bd in ((w_rg, wrg_bd), (w_ig, wig_bd)):
                v = w.rearrange("(j two) i o -> two i j o", two=2)
                for h in range(2):
                    g.dma_start(bd[HD * h:HD * h + HD, :, HD * h:HD * h + HD], v[h]).then_inc(gatew_loaded, 16)
            link(g.memset(pick[:, :], 0.0))
            for r0 in range(0, P, N_EXP):
                ins = g.affine_select(out=pick[:, 0:N_EXP], in_=pick[:, 0:N_EXP], compare_op=ALU.not_equal, fill=1.0, base=-r0,
                                      pattern=[[-1, N_EXP]], channel_multiplier=1)
                if r0 < P - N_EXP:
                    link(ins)
                else:
                    ins.then_inc(pick_ready, 1)
            link(g.memset(same_half[:, :], 0.0))
            for h in (0, SLOTS):
                g.memset(same_half[h:h + SLOTS, h:h + SLOTS], 1.0).then_inc(pick_ready, 1)
                g.wait_ge(pick_ready, 2 + h // SLOTS)
            link(g.memset(causal[:, :], 0.0))
            for k0 in (0, 2 * P):
                g.affine_select(out=causal[:, k0:k0 + P], in_=causal[:, k0:k0 + P], compare_op=ALU.is_ge, fill=MASKED,
                                base=0, pattern=[[-1, P]], channel_multiplier=1).then_inc(causal_ready, 1)
            link(g.memset(neg8[:, :], 0.0))
            link(g.affine_select(out=neg8[:, :], in_=neg8[:, :], compare_op=ALU.not_equal, fill=-math.sqrt(HD), base=0,
                                 pattern=[[-1, HEADS]], channel_multiplier=1))
            g.affine_select(out=neg8[:, :], in_=neg8[:, :], compare_op=ALU.not_equal, fill=-math.sqrt(HD), base=-F_REST,
                            pattern=[[-1, HEADS]], channel_multiplier=1).then_inc(neg8_ready, 1)
            g.iota(iota[:, :, :], pattern=[[0, 2], [1, SLOTS]], base=0, channel_multiplier=0,
                   allow_small_or_imprecise_dtypes=True).then_inc(iota_ready, 1)

            def split_upper(c):
                g.wait_ge(hi_ready, c + 1)
                src = ring[:, c % MIX_RING, :].rearrange("p (k n) -> p k n", k=KT)
                g.tensor_tensor(w_lo[c % 2][:, KT // 2:, :], src[:, KT // 2:, :], w_hi[c % 2][:, KT // 2:, :].bitcast(F32),
                                ALU.subtract).then_inc(lo_pool_ready, 1)

            for c in range(30):
                split_upper(c)
            g.wait_ge(ylru_ready, 1)
            g.dma_start(gffn_b, g_ffn.rearrange("(a n) -> a n", a=1).broadcast_to([P, D])).then_inc(late_loaded, 16)
            g.dma_start(bdn, b_down[:, :]).then_inc(late_loaded, 16)
            g.wait_ge(o_hi_ready, 1)
            g.tensor_tensor(hT_lo[:, 0:6, :], Q[:, 0:6, :], hT_hi[:, 0:6, :].bitcast(F32), ALU.subtract).then_inc(o_lo_ready, 1)
            for c in range(30, 34):
                split_upper(c)
            g.wait_ge(s_psum, HEADS)
            for i in range(4):
                g.dma_start(bgu_raw[i * N_EXP:(i + 1) * N_EXP, :].rearrange("e (q n) -> e q n", q=2),
                            b_gate_up.rearrange("e (q h n) -> h e q n", q=2, h=2)[i // 2]).then_inc(late_loaded, 16)
            g.wait_ge(o_psum, HEADS)
            g.memset(ones, 1.0).then_inc(ones_ready, 1)
            g.wait_ge(ones_ready, 1)
            g.affine_select(out=tri, in_=ones, compare_op=ALU.is_gt, fill=0.0, base=0,
                            pattern=[[1, P]], channel_multiplier=-1).then_inc(tri_ready, 1)
            for c in range(34, MIX_CHUNKS):
                split_upper(c)
            g.wait_ge(bgu_part_ready, 1)
            g.tensor_tensor(bgu[:, :], bgu_raw, bgu_part[:, :].bitcast(F32), ALU.subtract).then_inc(bgu_split, 1)
            g.wait_ge(h2_scaled, 1)
            g.tensor_tensor(h2[:, 0, :], h2[:, 0, :], gffn_b, ALU.mult).then_inc(h2_ready[0], 1)
            g.wait_ge(chunk_done, MIX_CHUNKS + GU_CHUNKS)
            g.dma_start(gfin_b, g_final.rearrange("(a n) -> a n", a=1).broadcast_to([P, D])).then_inc(gfin_loaded, 16)

        @block.scalar
        def _(act):
            steps = [0]

            def link(ins):
                steps[0] += 1
                ins.then_inc(act_step, 1)
                act.wait_ge(act_step, steps[0])

            act.wait_ge(x_loaded[0], 16)
            act.activation(lru_pad[:, 0:4, 0:S], x_sb[:, 0, :].rearrange("p (a b) -> p a b", a=4), ACT.Square,
                           accum_out=stat[:, 0:1]).then_inc(sumsq_ready, 1)
            act.wait_ge(sumsq_ready, TT)
            act.wait_ge(eps_ready, 1)
            act.activation(stat[:, 2:4], stat[:, 0:2], ACT.Sqrt, scale=1.0 / D, bias=epsc[:, 0:1]).then_inc(rms_ready, 1)

            def evac(c):
                g, j = c // 4 * 4, c % 4
                act.wait_ge(chunk_done, c + 1)
                src = pj[c % 2][:, :].rearrange("p (a s) -> p a s", a=2)
                if g == C_V:
                    dst = V[:, :, j * CC:(j + 1) * CC]
                elif g == C_LRU:
                    dst = lru_pad[:, 2 * j:2 * j + 2, CONV - 1:]
                else:
                    dst = {C_K: K, C_Q: Q, C_LG: LG, C_GL: GL, C_GF: GF}[g][:, 2 * j:2 * j + 2, :]
                act.activation(dst, src, ACT.Identity).then_inc(act_evac, 1)

            def split(c):
                act.wait_ge(loaded[c % MIX_RING], 16 * (c // MIX_RING + 1))
                if c >= 2:
                    act.wait_ge(chunk_done, c - 1)
                act.activation(w_hi[c % 2][:, :, :], ring[:, c % MIX_RING, :].rearrange("p (k n) -> p k n", k=KT),
                               ACT.Identity).then_inc(hi_ready, 1)

            def after_chunk(c):
                if c + 2 < MIX_CHUNKS:
                    split(c + 2)
                if c < C_WL:
                    evac(c)

            split(0)
            for j in range(4):
                act.wait_ge(hT32_ready, 2 * j + 2)
                act.activation(hT_hi[:, 2 * j:2 * j + 2, :], hT32[:, 2 * j:2 * j + 2, :], ACT.Identity).then_inc(hT_hi_ready, 1)
            split(1)
            for c in range(4):
                after_chunk(c)
            act.wait_ge(f_psum, 1)
            act.wait_ge(small_loaded, 96)
            link(act.activation(fz[:, 0, :], ga[0:F_ROWS, 0:S], ACT.Identity, bias=bf[:, 0:1]))
            link(act.activation(fz[:, 1, :], fz[:, 0, :], ACT.Abs))
            act.activation(fz[:, 2, :], fz[:, 1, :], ACT.Exp, scale=-1.0).then_inc(f_exp, 1)
            act.wait_ge(lam_abs, 1)
            act.activation(lam[:, 1, :], lam[:, 0, :], ACT.Exp, scale=-1.0).then_inc(lam_exp, 1)
            for j in range(KT):
                after_chunk(C_K + j)
                act.wait_ge(gates_psum, j + 1)
                b = (ga, gb)[j % 2]
                act.activation(R[:, j, :], b[:, 0:S], ACT.Sigmoid, bias=vec[:, V_BRG + j:V_BRG + j + 1]).then_inc(ri_ready, 1)
                act.activation(I[:, j, :], b[:, S:2 * S], ACT.Sigmoid, bias=vec[:, V_BIG + j:V_BIG + j + 1]).then_inc(ri_ready, 1)
            act.wait_ge(loga_ready, KT)
            act.activation(mult, R[:, :, :], ACT.Tanh).then_inc(tanh_ready, 1)
            act.activation(a_sq, R[:, :, :], ACT.Exp, scale=2.0).then_inc(tanh_ready, 1)
            act.wait_ge(tanh_ready, 2)
            act.activation(R[:, :, :], R[:, :, :], ACT.Exp).then_inc(a_ready, 1)

            for s in range(HEADS + 2):
                if s >= 1:
                    after_chunk(C_V - 1 + s)
                if s < HEADS:
                    act.wait_ge(logits_ready, s + 1)
                    for q, (lo, hi) in enumerate(((0, P), (P, 3 * P))):
                        n = 2 * (s % 2) + q
                        act.activation(L[:, s % 2, lo:hi], L[:, s % 2, lo:hi], ACT.Exp, scale=1 / math.sqrt(HD),
                                       bias=stat[:, 8 + n:9 + n], accum_out=stat[:, 12 + n:13 + n]).then_inc(exp_ready, 1)
                if s % 2 == 0 and s >= 4:
                    j = s // 2 - 2
                    act.wait_ge(o_psum, 2 * j + 2)
                    act.activation(Q[:, j, :], ob[j % 2][:, 0:S], ACT.Identity).then_inc(o_evac, 1)
                if s == 2:
                    act.wait_ge(mult2_ready, 1)
                    act.activation(mult, mult, ACT.Sqrt, scale=-1.0).then_inc(mult_ready, 1)
                if s == 8:
                    act.wait_ge(act_evac, C_LG + 4)
                    act.activation(LG[:, :, :], LG[:, :, :], ACT.Gelu_apprx_tanh).then_inc(gelu_ready, 1)
                if s == 10:
                    act.wait_ge(ylru_ready, 1)
                    act.wait_ge(scans_done, 1)
                    act.activation(y_hi[:, :, :], XC[:, :, :], ACT.Identity).then_inc(y_hi_ready, 1)
                if s == 12:
                    act.wait_ge(act_evac, C_GL + 4)
                    act.activation(GL[:, :, :], GL[:, :, :], ACT.Sigmoid).then_inc(gl_ready, 1)
                if s == 16:
                    act.wait_ge(act_evac, C_GF + 4)
                    act.activation(GF[:, :, :], GF[:, :, :], ACT.Sigmoid).then_inc(gf_ready, 1)
                    act.wait_ge(o_evac, 6)
                    act.activation(hT_hi[:, 0:6, :], Q[:, 0:6, :], ACT.Identity).then_inc(o_hi_ready, 1)
            act.wait_ge(o_psum, HEADS)
            act.activation(Q[:, KT - 1, :], ob[1][:, 0:S], ACT.Identity).then_inc(o_evac, 1)
            act.wait_ge(o_evac, KT)
            act.activation(hT_hi[:, 6:8, :], Q[:, 6:8, :], ACT.Identity).then_inc(o_hi_ready, 1)
            for c in range(C_V + HEADS + 1, C_WF):
                after_chunk(c)
            act.wait_ge(y_lo_ready, 1)
            for j in range(4):
                if j < 3:
                    after_chunk(C_WF + j)
                act.wait_ge(chunk_done, C_WF + j + 1)
                act.wait_ge(merged_ready, j + 1)
                act.activation(y_hi[:, 2 * j:2 * j + 2, :], mg[:, 2 * j:2 * j + 2, :], ACT.Identity).then_inc(m_hi_ready, 1)
            after_chunk(C_WF + 3)

            for c in range(4):
                if C_WO + c + 2 < MIX_CHUNKS:
                    split(C_WO + c + 2)
                act.wait_ge(dve_evac, C_WO - C_WL + c + 1)
                for t in range(TT):
                    act.activation(sq[t][:, c * CC:(c + 1) * CC], x_sb[:, t, c * CC:(c + 1) * CC], ACT.Square,
                                   accum_out=stat[:, 48 + 4 * t + c:49 + 4 * t + c]).then_inc(sumsq2, 1)
                if c == 2:
                    act.wait_ge(late_loaded, 96)
                    act.wait_ge(rest_row_ready, 4)
                    act.activation(bgu_part[:, :], bgu_raw, ACT.Identity, scale=rest_row[:, 0:1]).then_inc(bgu_part_ready, 1)
                act.wait_ge(h2T_psum, c + 1)
                act.activation(h2T[:, 2 * c:2 * c + 2, :].rearrange("p a b -> p (a b)"), acc[c // 2][c % 2][:, :],
                               ACT.Identity).then_inc(h2T_ready, 1)
            act.wait_ge(sumsq2_ready, 1)
            act.activation(stat[:, 22:24], stat[:, 20:22], ACT.Sqrt, scale=1.0 / D, bias=epsc[:, 0:1]).then_inc(rms2, 1)
            act.wait_ge(rs2_ready, 1)
            act.activation(h2[:, 0, :], x_sb[:, 0, :], ACT.Identity, scale=stat[:, 26:27]).then_inc(h2_scaled, 1)
            for t in range(TT):
                act.wait_ge(neg_top, 1)
                act.activation(expw[:, t, :], lg[:, t, TOP_K:], ACT.Exp, bias=stat[:, 30 + t:31 + t]).then_inc(exp_top, 1)
            def expert_round(b0, n0, t0, first=False):
                def hg_copy(b):
                    act.wait_ge(gathered, b + 1)
                    act.activation(hg[:, 0:KT // 2, :, :], ga[:, :].rearrange("p (k i s) -> p k i s", i=2, s=SLOTS),
                                   ACT.Identity).then_inc(hg_ready, 1)

                def sigmoid_of(n):
                    act.wait_ge(gate_ready, n + 1)
                    act.activation(sig, gate, ACT.Sigmoid, scale=ALPHA).then_inc(sig_ready, 1)

                def moves_of(n):
                    act.wait_ge(act_transposed, n + 1)
                    act.activation(actT, ga[:, :].rearrange("p (j h s) -> p j h s", h=2, s=SLOTS), ACT.Identity).then_inc(actT_ready, 1)
                    act.wait_ge(chunk_done, n * EXP_CHUNKS + MIX_CHUNKS + EXP_CHUNKS)
                    act.activation(Y, gb[:, :], ACT.Identity).then_inc(y_ready, 1)

                hg_copy(b0)
                if first:
                    act.wait_ge(combT_psum, 1)
                    act.activation(combT, pt[0:N_EXP, 0:S], ACT.Identity).then_inc(combT_ready, 1)
                with act.Fori(0, PAIRS) as p:
                    n = p * 2 + n0
                    sigmoid_of(n)
                    act.wait_ge(selw_transposed, p + t0 + 1)
                    act.activation(selWT, gb[:, :].rearrange("p (i n) -> p i n", i=2), ACT.Identity).then_inc(selwt_ready, 1)
                    moves_of(n)
                    sigmoid_of(n + 1)
                    hg_copy(p + b0 + 1)
                    moves_of(n + 1)

            expert_round(0, 0, 0, True)
            act.wait_ge(flag_ready, 1)
            over = act.value_load(flag_i[0:1, 0:1], min_val=0, max_val=1)
            with act.If(over > 0):
                with act.Fori(1, ROUNDS) as r:
                    expert_round(r * (PAIRS + 1), r * N_EXP, r * PAIRS)
            act.end_ifs()

            act.activation(stat[:, 60:61], epsc[:, 0:1], ACT.Sqrt).then_inc(rms3, 1)
            for t in range(TT):
                for h in range(2):
                    act.wait_ge(y_summed, 2 * t + h + 1)
                    act.activation(h2[:, t, h * 512:(h + 1) * 512], yo[:, t, h * 512:(h + 1) * 512], ACT.Square,
                                   accum_out=stat[:, 40 + 2 * t + h:41 + 2 * t + h]).then_inc(sumsq3, 1)
                act.wait_ge(sum3_ready, t + 1)
                act.activation(stat[:, 64 + t:65 + t], stat[:, 66 + t:67 + t], ACT.Sqrt, scale=1.0 / D,
                               bias=epsc[:, 0:1]).then_inc(rms3, 1)

        @block.vector
        def _(dve):
            v = nc.vector
            steps = [0]

            def link(ins):
                steps[0] += 1
                ins.then_inc(dve_step, 1)
                dve.wait_ge(dve_step, steps[0])

            v.memset(epsc[:, :], RMS_EPS).then_inc(eps_ready, 1)
            v.memset(wf[:, :, HEADS:F_REST], 0.0).then_inc(f_zeroed, 1)
            v.memset(bf[:, :], 0.0).then_inc(f_zeroed, 1)
            for i in range(4):
                v.memset(rest_row[i * N_EXP:(i + 1) * N_EXP, :], float(i % 2)).then_inc(rest_row_ready, 1)
            dve.wait_ge(rest_row_ready, 4)
            dve.wait_ge(x_loaded[1], 16)
            v.tensor_tensor_reduce(out=flat(XC)[:, 0:D], in0=x_sb[:, 1, :], in1=x_sb[:, 1, :], scale=1.0, scalar=0.0,
                                   op0=ALU.mult, op1=ALU.add, accum_out=stat[:, 1:2]).then_inc(sumsq_ready, 1)
            dve.wait_ge(rms_ready, 1)
            link(v.reciprocal(stat[:, 4:6], stat[:, 2:4]))
            for t in range(TT):
                v.tensor_scalar(xs[:, t, :], x_sb[:, t, :], stat[:, 4 + t:5 + t], None, ALU.mult).then_inc(xs_ready, 1)
            v.memset(lru_pad[:, :, 0:CONV - 1], 0.0).then_inc(pad_ready, 1)
            dve.wait_ge(vec_psum, 1)
            v.tensor_copy(vec[:, :], ga[:, 0:NVEC]).then_inc(vec_ready, 1)
            dve.wait_ge(vec_ready, 1)
            dve.wait_ge(sumsq_ready, TT)

            def split_lower(c):
                dve.wait_ge(hi_ready, c + 1)
                src = ring[:, c % MIX_RING, :].rearrange("p (k n) -> p k n", k=KT)
                v.tensor_tensor(w_lo[c % 2][:, 0:KT // 2, :], src[:, 0:KT // 2, :], w_hi[c % 2][:, 0:KT // 2, :].bitcast(F32),
                                ALU.subtract).then_inc(lo_dve_ready, 1)

            def hT_rest(j):
                dve.wait_ge(hT_hi_ready, j + 1)
                v.tensor_tensor(hT_lo[:, 2 * j:2 * j + 2, :], hT32[:, 2 * j:2 * j + 2, :],
                                hT_hi[:, 2 * j:2 * j + 2, :].bitcast(F32), ALU.subtract).then_inc(hT_lo_ready, 1)

            split_lower(0)
            for j in range(KT):
                dve.wait_ge(hT_psum, j // 2 + 1)
                v.tensor_scalar(hT32[:, j, :], (ps[0], ps[1], pt, po)[j // 2][:, S * (j % 2):S * (j % 2) + S],
                                vec[:, V_GMIX + j:V_GMIX + j + 1], None, ALU.mult).then_inc(hT32_ready, 1)
                if j in (3, 5, 7):
                    hT_rest(j // 2 - 1)
            hT_rest(3)
            split_lower(1)
            link(v.scalar_tensor_tensor(lam[:, 0, :], vec[:, V_LAM:V_LAM + KT], -1.0, vec[:, V_LAM:V_LAM + KT], ALU.mult, ALU.max))
            v.tensor_copy(lam[:, 1, :], lam[:, 0, :]).then_inc(lam_abs, 1)
            dve.wait_ge(small_loaded, 96)
            v.tensor_tensor(wr[:, :, :], wr[:, :, :], vec[:, V_GFFN:V_GFFN + KT].unsqueeze(2).broadcast_to([P, KT, N_EXP]),
                            ALU.mult).then_inc(wr_ready, 1)
            dve.wait_ge(pad_ready, 1)
            dve.wait_ge(f_psum, 1)
            for c in range(4):
                split_lower(c + 2)
                dve.wait_ge(act_evac, C_LRU + c + 1)
                for i in range(CONV):
                    for j in (2 * c, 2 * c + 1):
                        w1 = vec[:, V_CONVW + i * KT + j:V_CONVW + i * KT + j + 1]
                        if i == 0:
                            ins = v.tensor_scalar(XC[:, j, :], lru_pad[:, j, 0:S], w1, vec[:, V_CONVB + j:V_CONVB + j + 1],
                                                  ALU.mult, ALU.add)
                        else:
                            ins = v.scalar_tensor_tensor(XC[:, j, :], lru_pad[:, j, i:i + S], w1, XC[:, j, :],
                                                         ALU.mult, ALU.add)
                        if i == CONV - 1:
                            ins.then_inc(conv_ready, 1)
                        elif j % 2:
                            link(ins)
                        else:
                            ins.then_inc(conv_even, 1)
                    if i < CONV - 1:
                        dve.wait_ge(conv_even, (CONV - 1) * c + i + 1)

            def half_log1p(e, y, w, q):
                link(v.tensor_scalar(w, e, 2.0, None, ALU.add))
                link(v.reciprocal(w, w))
                link(v.tensor_tensor(y, e, w, ALU.mult))
                link(v.tensor_tensor(w, y, y, ALU.mult))
                link(v.tensor_scalar(q, w, 1.0 / 15.0, None, ALU.mult))
                for k in (13, 11, 9, 7, 5, 3):
                    link(v.scalar_tensor_tensor(q, q, 1.0 / k, w, ALU.add, ALU.mult))
                link(v.scalar_tensor_tensor(q, q, 1.0, y, ALU.add, ALU.mult))

            dve.wait_ge(lam_exp, 1)
            half_log1p(lam[:, 1, :], lam[:, 2, :], lam[:, 3, :], lam[:, 4, :])
            link(v.tensor_scalar(lam[:, 2, :], vec[:, V_LAM:V_LAM + KT], 0.0, LRU_C, ALU.min, ALU.mult))
            link(v.scalar_tensor_tensor(lam[:, 0, :], lam[:, 4, :], -2.0 * LRU_C, lam[:, 2, :], ALU.mult, ALU.add))
            split_lower(6)
            dve.wait_ge(f_exp, 1)
            half_log1p(fz[:, 2, :], fz[:, 3, :], fz[:, 4, :], fz[:, 5, :])
            split_lower(7)
            link(v.tensor_scalar(fz[:, 3, :], fz[:, 0, :], 0.0, None, ALU.min))
            link(v.scalar_tensor_tensor(fz[:, 4, :], fz[:, 5, :], -2.0, fz[:, 3, :], ALU.mult, ALU.add))
            link(v.memset(fz[:, 6, :], 1.0))
            link(v.tensor_tensor_scan(cumf, fz[:, 6, :], fz[:, 4, :], 0.0, ALU.mult, ALU.add))
            link(v.tensor_scalar(cumf_part[:, :], cumf, rest_row[0:F_ROWS, 0:1], None, ALU.mult))
            dve.wait_ge(neg8_ready, 1)
            link(v.tensor_copy(neg8_r[:, :], neg8[:, :]))
            v.tensor_tensor(cumf_r[:, :], cumf, cumf_part[:, :].bitcast(F32), ALU.subtract).then_inc(cum_ready, 1)
            for j in range(KT):
                if j >= 2:
                    split_lower(C_K + 2 + j)
                dve.wait_ge(ri_ready, 2 * j + 1)
                v.tensor_scalar(R[:, j, :], R[:, j, :], lam[:, 0, j:j + 1], None, ALU.mult).then_inc(loga_ready, 1)
            dve.wait_ge(cum_ready, 1)

            def merge_lru(c):
                dve.wait_ge(gl_ready, 1)
                dve.wait_ge(chunk_done, C_WL + c + 1)
                v.tensor_tensor(mg[:, 2 * c:2 * c + 2, :], pj[c % 2][:, :].rearrange("p (a s) -> p a s", a=2),
                                GL[:, 2 * c:2 * c + 2, :], ALU.mult).then_inc(dve_evac, 1)

            for s in range(HEADS + 2):
                if 1 <= s <= HEADS:
                    b = (s - 1) % 2
                    dve.wait_ge(exp_ready, 2 * s)
                    link(v.reciprocal(stat[:, 16 + 2 * b:18 + 2 * b], stat[:, 12 + 2 * b:14 + 2 * b]))
                    for q, (lo, hi) in enumerate(((0, P), (P, 3 * P))):
                        v.tensor_scalar(L[:, b, lo:hi], L[:, b, lo:hi], stat[:, 16 + 2 * b + q:17 + 2 * b + q], None,
                                        ALU.mult).then_inc(p_ready, 1)
                if s >= 2:
                    dve.wait_ge(pt_psum, s - 1)
                    if s >= 4:
                        dve.wait_ge(o_psum, s - 3)
                    v.tensor_copy(PT[:, s % 2, :], pt[:, 0:3 * P]).then_inc(pt_ready, 1)
                if s < HEADS:
                    if s == 0:
                        dve.wait_ge(causal_ready, 2)
                    dve.wait_ge(s_psum, s + 1)
                    link(v.tensor_tensor(L[:, s % 2, :], ps[s % 2][:, 0:3 * P], causal[:, :], ALU.add))
                    n = 2 * (s % 2)
                    link(v.reduce_max(stat[:, 24:25], L[:, s % 2, 0:P], AX.X))
                    link(v.reduce_max(stat[:, 25:26], L[:, s % 2, P:3 * P], AX.X))
                    v.tensor_scalar(stat[:, 8 + n:10 + n], stat[:, 24:26], -1.0 / math.sqrt(HD), None,
                                    ALU.mult).then_inc(logits_ready, 1)
                    dve.wait_ge(logits_ready, s + 1)
                if s >= 1:
                    split_lower(C_V + 1 + s)
                if s == 0:
                    dve.wait_ge(tanh_ready, 2)
                    v.scalar_tensor_tensor(mult, a_sq, 1.0, mult, ALU.add, ALU.mult).then_inc(mult2_ready, 1)
                if s == 1:
                    dve.wait_ge(ri_ready, 2 * KT)
                    dve.wait_ge(conv_ready, KT)
                    link(v.tensor_tensor(I[:, :, :], I[:, :, :], XC[:, :, :], ALU.mult))
                if s == 3:
                    dve.wait_ge(mult_ready, 1)
                    link(v.tensor_tensor(I[:, :, :], I[:, :, :], mult, ALU.mult))
                if 4 <= s <= 7:
                    dve.wait_ge(a_ready, 1)
                    for j in (2 * s - 8, 2 * s - 7):
                        ins = v.tensor_tensor_scan(XC[:, j, :], R[:, j, :], I[:, j, :], 0.0, ALU.mult, ALU.add)
                        if j < KT - 1:
                            link(ins)
                    if s == 7:
                        ins.then_inc(scans_done, 1)
                if s == 9:
                    dve.wait_ge(scans_done, 1)
                    dve.wait_ge(gelu_ready, 1)
                    v.tensor_tensor(XC[:, :, :], XC[:, :, :], LG[:, :, :], ALU.mult).then_inc(ylru_ready, 1)
                if s == 11:
                    dve.wait_ge(ylru_ready, 1)
                    dve.wait_ge(y_hi_ready, 1)
                    v.tensor_tensor(y_lo[:, :, :], XC[:, :, :], y_hi[:, :, :].bitcast(F32), ALU.subtract).then_inc(y_lo_ready, 1)
                    dve.wait_ge(y_lo_ready, 1)
                if s == HEADS + 1:
                    merge_lru(0)

            split_lower(31)
            merge_lru(1)
            dve.wait_ge(o_hi_ready, 2)
            v.tensor_tensor(hT_lo[:, 6:8, :], Q[:, 6:8, :], hT_hi[:, 6:8, :].bitcast(F32), ALU.subtract).then_inc(o_lo_ready, 1)
            for c in range(2, 4):
                split_lower(C_WL + c + 2)
                merge_lru(c)
            for c in range(4):
                dve.wait_ge(gf_ready, 1)
                dve.wait_ge(chunk_done, C_WF + c + 1)
                v.tensor_tensor(tmp, pj[c % 2][:, :].rearrange("p (a s) -> p a s", a=2),
                                GF[:, 2 * c:2 * c + 2, :], ALU.mult).then_inc(dve_evac, 1)
                dve.wait_ge(dve_evac, 4 + c + 1)
                v.tensor_tensor(mg[:, 2 * c:2 * c + 2, :], mg[:, 2 * c:2 * c + 2, :], tmp, ALU.add).then_inc(merged_ready, 1)
                dve.wait_ge(merged_ready, c + 1)
                if c < 3:
                    split_lower(C_WF + c + 2)
                dve.wait_ge(m_hi_ready, c + 1)
                v.tensor_tensor(y_lo[:, 2 * c:2 * c + 2, :], mg[:, 2 * c:2 * c + 2, :],
                                y_hi[:, 2 * c:2 * c + 2, :].bitcast(F32), ALU.subtract).then_inc(m_lo_ready, 1)
            split_lower(C_WO + 1)
            for c in range(4):
                if C_WO + c + 2 < MIX_CHUNKS:
                    split_lower(C_WO + c + 2)
                dve.wait_ge(chunk_done, C_WO + c + 1)
                v.tensor_tensor(x_sb[:, :, c * CC:(c + 1) * CC], x_sb[:, :, c * CC:(c + 1) * CC],
                                pj[c % 2][:, :].rearrange("p (a s) -> p a s", a=2), ALU.add).then_inc(dve_evac, 1)

            link(v.memset(lg[:, :, 0:TOP_K], BIG))
            link(v.memset(comb[:, :, N_EXP:], 0.0))
            link(v.memset(pos[:, :, :], -1.0))
            dve.wait_ge(sumsq2, 8)
            v.tensor_reduce(stat[:, 20:22], stat[:, 48:56].rearrange("p (t c) -> p t c", t=TT), AX.X, ALU.add).then_inc(sumsq2_ready, 1)
            dve.wait_ge(rms2, 1)
            v.reciprocal(stat[:, 26:28], stat[:, 22:24]).then_inc(rs2_ready, 1)
            dve.wait_ge(rs2_ready, 1)

            dve.wait_ge(router_psum, 1)
            for t in range(TT):
                link(v.scalar_tensor_tensor(lg[:, t, TOP_K:], ga[:, t * N_EXP:(t + 1) * N_EXP], stat[:, 26 + t:27 + t],
                                            brt[:, :], ALU.mult, ALU.add))
            for t in range(TT):
                link(v.max(top8[:, t, :], lg[:, t, :]))
            v.tensor_scalar(stat[:, 30:32], top8[:, :, TOP_K], -1.0, None, ALU.mult).then_inc(neg_top, 1)
            for t in range(TT):
                link(v.match_replace(rep[:, t, :], top8[:, t, :], lg[:, t, :], -BIG))
            v.tensor_tensor(msk, rep[:, :, TOP_K:], lg[:, :, TOP_K:], ALU.not_equal).then_inc(mask_ready, 1)
            dve.wait_ge(mask_ready, 1)
            dve.wait_ge(late_loaded, 96)
            v.scalar_tensor_tensor(h2[:, 1, :], x_sb[:, 1, :], stat[:, 27:28], gffn_b, ALU.mult, ALU.mult).then_inc(h2_ready[1], 1)
            dve.wait_ge(pos_psum, 1)
            link(v.scalar_tensor_tensor(pos[:, :, 0:N_EXP], ga[:, 256:256 + TT * N_EXP].rearrange("p (t e) -> p t e", t=TT),
                                        1.0, msk, ALU.add, ALU.mult))
            link(v.tensor_scalar(pos[:, :, 0:N_EXP], pos[:, :, 0:N_EXP], -1.0, None, ALU.add))

            def combine_weights():
                dve.wait_ge(exp_top, TT)
                link(v.tensor_tensor(expw, expw, msk, ALU.mult))
                link(v.reduce_sum(stat[:, 32:34], expw, AX.X))
                link(v.reciprocal(stat[:, 34:36], stat[:, 32:34]))
                v.tensor_tensor(comb[:, :, 0:N_EXP], expw, stat[:, 34:36].unsqueeze(2).broadcast_to([P, TT, N_EXP]),
                                ALU.mult).then_inc(comb_ready, 1)
                dve.wait_ge(comb_ready, 1)

            def find_overflow():
                dve.wait_ge(maxT_psum, 1)
                link(v.reduce_max(flag[0:1, 0:1], po[0:1, 0:P], AX.X))
                link(v.tensor_scalar(flag[0:1, 1:2], flag[0:1, 0:1], float(SLOTS) - 0.5, None, ALU.is_gt))
                v.tensor_copy(flag_i[0:1, 0:1], flag[0:1, 1:2]).then_inc(flag_ready, 1)

            def build_sel(e):
                v.tensor_tensor(sel, iota[:, :, :].rearrange("p a s -> p (a s)").unsqueeze(1).unsqueeze(1).broadcast_to([P, TT, 2, P])
                                , pos[:, :, bass.ds(e, 2)].unsqueeze(3).broadcast_to([P, TT, 2, P]),
                                ALU.is_equal).then_inc(sel_ready, 1)

            def weigh_sel(e):
                v.tensor_tensor(selW, sel, comb[:, :, bass.ds(e, 2)].unsqueeze(3).broadcast_to([P, TT, 2, P]),
                                ALU.mult).then_inc(sel_ready, 1)

            def build_onehot(e):
                v.tensor_tensor(onehot[:, :, :], pick[:, bass.ds(e, 2)].unsqueeze(2).broadcast_to([P, 2, P]),
                                same_half[:, :].unsqueeze(1).broadcast_to([P, 2, P]), ALU.mult).then_inc(onehot_ready, 1)

            dve.wait_ge(iota_ready, 1)
            dve.wait_ge(pick_ready, 3)

            def expert_round(b0, n0, t0, first=False):
                def glu_of(n):
                    c0 = n * 2
                    dve.wait_ge(chunk_done, n * EXP_CHUNKS + MIX_CHUNKS + GU_CHUNKS)
                    v.tensor_scalar(gate, pj[0][:, :], LIMIT, None, ALU.min).then_inc(gate_ready, 1)
                    v.tensor_scalar(up, pj[1][:, :], LIMIT, -LIMIT, ALU.min, ALU.max).then_inc(moe_step, 1)
                    dve.wait_ge(gate_ready, n + 1)
                    dve.wait_ge(sig_ready, n + 1)
                    v.tensor_tensor(glu, gate, sig, ALU.mult).then_inc(moe_step, 1)
                    dve.wait_ge(moe_step, c0 + 2)
                    v.scalar_tensor_tensor(prod, up, 1.0, glu, ALU.add, ALU.mult).then_inc(act_ready, 1)

                def hg_copy(b):
                    dve.wait_ge(gathered, b + 1)
                    v.tensor_copy(hg[:, KT // 2:, :, :], gb[:, :].rearrange("p (k i s) -> p k i s", i=2, s=SLOTS)).then_inc(hg_ready, 1)

                build_sel(0)
                build_onehot(0)
                if first:
                    combine_weights()
                    v.tensor_reduce(stat[:, 36:37], pos[:, :, :], AX.XY, ALU.max).then_inc(maxp_ready, 1)
                dve.wait_ge(sel_ready, b0 * 2 + 1)
                weigh_sel(0)
                hg_copy(b0)
                if first:
                    find_overflow()
                with dve.Fori(0, PAIRS) as p:
                    n, t, e = p * 2 + n0, p + t0, p * 2 + 2
                    glu_of(n)
                    dve.wait_ge(gathered, p + b0 + 1)
                    build_sel(e)
                    dve.wait_ge(selw_transposed, t + 1)
                    dve.wait_ge(sel_ready, (p + b0) * 2 + 3)
                    weigh_sel(e)
                    glu_of(n + 1)
                    build_onehot(e)
                    hg_copy(p + b0 + 1)

            expert_round(0, 0, 0, True)
            dve.wait_ge(flag_ready, 1)
            over = dve.value_load(flag_i[0:1, 0:1], min_val=0, max_val=1)
            with dve.If(over > 0):
                dve.wait_ge(scattered, TT * N_EXP)
                with dve.Fori(1, ROUNDS) as r:
                    dve.wait_ge(gathered, r * (PAIRS + 1))
                    v.tensor_scalar(pos[:, :, 0:N_EXP], pos[:, :, 0:N_EXP], -float(SLOTS), None,
                                    ALU.add).then_inc(moe_round, 1)
                    dve.wait_ge(moe_round, r)
                    expert_round(r * (PAIRS + 1), r * N_EXP, r * PAIRS)
                    dve.wait_ge(scattered, r * (TT * N_EXP) + TT * N_EXP)
            dve.end_ifs()

            for t in range(TT):
                dve.wait_ge(scattered, TT * N_EXP - 1 + t)
                for h in range(2):
                    v.tensor_tensor(yo[:, t, h * 512:(h + 1) * 512], x_sb[:, t, h * 512:(h + 1) * 512], acc[t][h][:, :],
                                    ALU.add).then_inc(y_summed, 1)
            dve.wait_ge(gfin_loaded, 16)
            for t in range(TT):
                dve.wait_ge(sumsq3, 2 * t + 2)
                v.tensor_tensor(stat[:, 66 + t:67 + t], stat[:, 40 + 2 * t:41 + 2 * t], stat[:, 41 + 2 * t:42 + 2 * t],
                                ALU.add).then_inc(sum3_ready, 1)
                dve.wait_ge(rms3, t + 2)
                link(v.reciprocal(stat[:, 44 + t:45 + t], stat[:, 64 + t:65 + t]))
                dve.wait_ge(y_summed, 2 * t + 2)
                v.scalar_tensor_tensor(yo[:, t, :], yo[:, t, :], stat[:, 44 + t:45 + t], gfin_b, ALU.mult,
                                       ALU.mult).then_inc(final_ready, 1)

        @block.tensor
        def _(pe):
            mm = nc.tensor.matmul

            pe.wait_ge(ident_ready, 1)
            pe.wait_ge(rows_loaded, 112)
            nc.tensor.transpose(ga[:, 0:NVEC], rows[:, :], ident[0:NVEC, 0:NVEC]).then_inc(vec_psum, 1)
            for j in range(KT):
                for t in range(TT):
                    if j == 0:
                        pe.wait_ge(xs_ready, t + 1)
                    c0 = S * (j % 2) + t * P
                    last = nc.tensor.transpose((ps[0], ps[1], pt, po)[j // 2][:, c0:c0 + P], xs[:, t, j * P:(j + 1) * P], ident[:, :])
                if j % 2:
                    last.then_inc(hT_psum, 1)
            def free_pj(c):
                if c - 2 >= C_WL:
                    pe.wait_ge(dve_evac, c - 1 - C_WL)
                elif c >= 2:
                    pe.wait_ge(act_evac, c - 1)

            def chunk(c):
                g = c // 4 * 4
                b = c % 2
                a_hi, a_lo = (y_hi, y_lo) if g in (C_WL, C_WO) else (hT_hi, hT_lo)
                pe.wait_ge(hi_ready, c + 1)
                pe.wait_ge(lo_dve_ready, c + 1)
                pe.wait_ge(lo_pool_ready, c + 1)
                free_pj(c)
                for a in range(2):
                    for k in range(KT):
                        if c == 0 and a == 0 and k % 2 == 0:
                            pe.wait_ge(hT_lo_ready, k // 2 + 1)
                        if c == C_WO and a == 0 and k % 2 == 0:
                            pe.wait_ge(m_hi_ready, k // 2 + 1)
                            pe.wait_ge(m_lo_ready, k // 2 + 1)
                        for n, (w, x_) in enumerate(((w_hi, a_hi), (w_hi, a_lo), (w_lo, a_hi))):
                            if g in (C_V, C_WO):
                                lhs, rhs = x_[:, k, a * P:(a + 1) * P], w[b][:, k, :]
                            else:
                                lhs, rhs = w[b][:, k, a * P:(a + 1) * P], x_[:, k, :]
                            last = mm(pj[b][:, a * S:(a + 1) * S], lhs, rhs, start=(k == 0 and n == 0),
                                      stop=(k == KT - 1 and n == 2))
                last.then_inc(chunk_done, 1)

            chunk(0)
            pe.wait_ge(hT32_ready, KT)
            pe.wait_ge(vec_ready, 1)
            pe.wait_ge(small_loaded, 96)
            for k in range(KT):
                last = mm(ga[0:F_ROWS, 0:S], wf[:, k, :], hT32[:, k, :], start=(k == 0), stop=(k == KT - 1))
            last.then_inc(f_psum, 1)
            for c in range(1, C_K):
                chunk(c)
            for j in range(KT):
                chunk(C_K + j)
                if j == 0:
                    pe.wait_ge(gatew_loaded, 64)
                pe.wait_ge(conv_ready, j + 1)
                if j >= 2:
                    pe.wait_ge(ri_ready, 2 * (j - 1))
                else:
                    pe.wait_ge(f_exp, 1)
                b = (ga, gb)[j % 2]
                mm(b[:, 0:S], wrg_bd[:, j, :], XC[:, j, :], start=True, stop=True)
                mm(b[:, S:2 * S], wig_bd[:, j, :], XC[:, j, :], start=True, stop=True).then_inc(gates_psum, 1)

            for s in range(HEADS + 2):
                if s < HEADS and s % 2 == 0:
                    if s == 0:
                        pe.wait_ge(cum_ready, 1)
                    if s % 4 == 0:
                        pe.wait_ge(act_evac, C_Q + s // 4 + 1)
                    if s >= 2:
                        pe.wait_ge(logits_ready, s)
                    j = s // 2
                    for q, (c0, n) in enumerate(((0, P), (P, 2 * P))):
                        for h in range(2):
                            r0 = HD * h
                            mm(ps[h][:, c0:c0 + n], Q[r0:r0 + HD, j, q * P:(q + 1) * P], K[r0:r0 + HD, j, 0:n],
                               start=True, stop=False)
                        for h in range(2):
                            last = mm(ps[h][:, c0:c0 + n], neg8_r[:, s + h:s + h + 1].broadcast_to([F_ROWS, P]), cumf_r[:, 0:n],
                                      start=False, stop=True)
                            if q == 1:
                                last.then_inc(s_psum, 1)
                if C_V + s == C_WL:
                    pe.wait_ge(y_hi_ready, 1)
                    pe.wait_ge(y_lo_ready, 1)
                chunk(C_V + s)
                if 1 <= s <= HEADS:
                    pe.wait_ge(p_ready, 2 * s)
                    if s >= 2:
                        pe.wait_ge(pt_ready, s - 1)
                    for b in range(3):
                        last = nc.tensor.transpose(pt[:, b * P:(b + 1) * P], L[:, (s - 1) % 2, b * P:(b + 1) * P], ident[:, :])
                    last.then_inc(pt_psum, 1)
                if s >= 3 and s % 2:
                    j = (s - 3) // 2
                    pe.wait_ge(pt_ready, 2 * j + 2)
                    if j % 2 == 0:
                        pe.wait_ge(act_evac, C_V + j // 2 + 1)
                    if j >= 2:
                        pe.wait_ge(o_evac, j - 1)
                    elif j == 1:
                        pe.wait_ge(ri_ready, 2 * KT)
                    for q, t, start in ((0, 0, True), (1, 0, True), (1, 1, False)):
                        for i in range(2):
                            last = mm(ob[j % 2][HD * i:HD * (i + 1), q * P:(q + 1) * P],
                                      V[:, t, (2 * j + i) * HD:(2 * j + i + 1) * HD], PT[:, i, (q + t) * P:(q + t + 1) * P],
                                      start=start, stop=(q == t))
                            if t == 1:
                                last.then_inc(o_psum, 1)
            for c in range(C_V + HEADS + 2, C_WF):
                chunk(c)
            pe.wait_ge(o_hi_ready, 2)
            pe.wait_ge(o_lo_ready, 2)
            for c in range(C_WF, C_WF + 4):
                chunk(c)
            def x2_transpose(c):
                pe.wait_ge(dve_evac, C_WO - C_WL + c + 1)
                for j in range(2):
                    for t in range(TT):
                        last = nc.tensor.transpose(acc[c // 2][c % 2][:, j * S + t * P:j * S + (t + 1) * P],
                                                   x_sb[:, t, (2 * c + j) * P:(2 * c + j + 1) * P], ident[:, :])
                last.then_inc(h2T_psum, 1)

            def route(c, t):
                for k in (2 * c, 2 * c + 1):
                    last = mm(ga[:, t * N_EXP:(t + 1) * N_EXP], h2T[:, k, t * P:(t + 1) * P], wr[:, k, :], start=(k == 0),
                              stop=(k == KT - 1))
                return last

            for c in range(4):
                chunk(C_WO + c)
                if c:
                    x2_transpose(c - 1)
            x2_transpose(3)
            pe.wait_ge(wr_ready, 1)
            for t in range(TT):
                for c in range(4):
                    pe.wait_ge(h2T_ready, c + 1)
                    last = route(c, t)
            last.then_inc(router_psum, 1)
            pe.wait_ge(tri_ready, 1)
            pe.wait_ge(mask_ready, 1)
            mm(ga[:, 256:256 + N_EXP], tri, msk[:, 0, :], start=True, stop=True)
            mm(ga[:, 256 + N_EXP:256 + 2 * N_EXP], ones, msk[:, 0, :], start=True, stop=False)
            mm(ga[:, 256 + N_EXP:256 + 2 * N_EXP], tri, msk[:, 1, :], start=False, stop=True).then_inc(pos_psum, 1)
            def transpose_combine():
                pe.wait_ge(comb_ready, 1)
                for t in range(TT):
                    last = nc.tensor.transpose(pt[0:N_EXP, t * P:(t + 1) * P], comb[:, t, 0:N_EXP], ident[:, :])
                last.then_inc(combT_psum, 1)
                pe.wait_ge(maxp_ready, 1)
                nc.tensor.transpose(po[0:1, 0:P], stat[:, 36:37], ident[:, :]).then_inc(maxT_psum, 1)

            def open_sums():
                pe.wait_ge(combT_ready, 1)
                pe.wait_ge(flag_ready, 1)
                for t in range(TT):
                    for h in range(2):
                        mm(acc[t][h][:, :], combT[:, t * P:(t + 1) * P], bdn[:, h * 512:(h + 1) * 512], start=True, stop=True,
                           skip_group_check=True)

            def expert_round(b0, n0, t0, first=False):
                def gather():
                    for k in range(KT):
                        for t in range(TT):
                            last = mm((ga, gb)[k // 4][:, k % 4 * P:(k % 4 + 1) * P], h2[:, t, k * P:(k + 1) * P],
                                      sel[:, t, :, 0:SLOTS], start=(t == 0), stop=(t == TT - 1))
                    last.then_inc(gathered, 1)

                def chunk_here(n, c, peeled):
                    if peeled and c in EXTRA:
                        pe.wait_ge(extra_loaded[c], 16)
                        return extra[c]
                    uses = MIX_CHUNKS // MIX_RING if c < MIX_RING else 0
                    pe.wait_ge(loaded[c], n * 16 + 16 * (uses + (c not in EXTRA)))
                    return ring[:, c, :]

                def gate_up(n, i, peeled=False):
                    for b in range(2):
                        mm(pj[b][:, :], onehot[:, i, :], bgu[:, b * 512:(b + 1) * 512], start=True, stop=False)
                    for c in range(GU_CHUNKS):
                        w = chunk_here(n, c, peeled)
                        for q in range(4):
                            h = SLOTS * (q % 2)
                            last = mm(pj[q // 2][h:h + SLOTS, :], hg[:, c, i, :], w[:, q * 512:(q + 1) * 512],
                                      start=False, stop=(c == GU_CHUNKS - 1))
                        last.then_inc(chunk_done, 1)

                def down(n, peeled=False):
                    pe.wait_ge(act_ready, n + 1)
                    for j in range(4):
                        last = nc.tensor.transpose(ga[:, j * P:(j + 1) * P], prod[:, j * P:(j + 1) * P], ident[:, :])
                    last.then_inc(act_transposed, 1)
                    pe.wait_ge(actT_ready, n + 1)
                    for c in range(DN_CHUNKS):
                        w = chunk_here(n, GU_CHUNKS + c, peeled)
                        for a in range(2):
                            f = 2 * c + a
                            for q in range(2):
                                h = SLOTS * q
                                last = mm(gb[h:h + SLOTS, :], actT[:, f % 4, f // 4, :],
                                          w[:, a * D + q * 512:a * D + (q + 1) * 512], start=(f == 0), stop=(f == KT - 1))
                        last.then_inc(chunk_done, 1)

                def scatter(n, i):
                    pe.wait_ge(y_ready, n + 1)
                    for t in range(TT):
                        for q in range(2):
                            h = SLOTS * q
                            last = mm(acc[t][q][:, :], selWT[h:h + SLOTS, i, t * P:(t + 1) * P], Y[h:h + SLOTS, :],
                                      start=False, stop=True, skip_group_check=True)
                        last.then_inc(scattered, 1)

                pe.wait_ge(sel_ready, b0 * 2 + 1)
                if first:
                    for t in range(TT):
                        pe.wait_ge(h2_ready[t], 1)
                gather()
                if first:
                    transpose_combine()
                    pe.wait_ge(bgu_split, 1)
                def pair(p, peeled=False):
                    n, b = p * 2 + n0, p + b0
                    pe.wait_ge(hg_ready, b * 2 + 2)
                    pe.wait_ge(onehot_ready, b + 1)
                    gate_up(n, 0, peeled)
                    pe.wait_ge(sel_ready, b * 2 + 2)
                    for i in range(2):
                        for t in range(TT):
                            last = nc.tensor.transpose(gb[:, (i * TT + t) * P:(i * TT + t + 1) * P], selW[:, t, i, :], ident[:, :])
                    last.then_inc(selw_transposed, 1)
                    if peeled:
                        open_sums()
                    pe.wait_ge(selwt_ready, p + t0 + 1)
                    down(n, peeled)
                    scatter(n, 0)
                    gate_up(n + 1, 1)
                    pe.wait_ge(sel_ready, b * 2 + 3)
                    gather()
                    pe.wait_ge(hg_ready, b * 2 + 4)
                    down(n + 1)
                    scatter(n + 1, 1)

                if first:
                    pair(0, True)
                with pe.Fori(int(first), PAIRS) as p:
                    pair(p)

            expert_round(0, 0, 0, True)
            over = pe.value_load(flag_i[0:1, 0:1], min_val=0, max_val=1)
            with pe.If(over > 0):
                with pe.Fori(1, ROUNDS) as r:
                    expert_round(r * (PAIRS + 1), r * N_EXP, r * PAIRS)
            pe.end_ifs()


_INS = ["x", "g_mix", "w_in", "conv_w", "conv_b", "w_rg", "b_rg", "w_ig", "b_ig", "lru_lambda", "b_f", "w_lru_out",
        "w_fox_out", "w_o", "g_ffn", "w_router", "b_router", "w_gate_up", "b_gate_up", "w_down", "b_down", "g_final"]


def kernel(**inputs):
    import concourse.bacc as bacc
    from concourse.bass_utils import run_bass_kernel_spmd

    nc = bacc.Bacc("TRN2", target_bir_lowering=False, num_devices=1)
    arrays, args = {}, []
    for name in _INS:
        a = np.ascontiguousarray(inputs[name])
        arrays[f"in_{name}"] = a
        args.append(nc.dram_tensor(f"in_{name}", a.shape, mybir.dt.from_np(a.dtype), kind="ExternalInput").ap())
    out = nc.dram_tensor("out_0", inputs["x"].shape, F32, kind="ExternalOutput").ap()
    hybrid_block(nc, *args, out)
    r = run_bass_kernel_spmd(nc, [arrays], core_ids=[0])
    return r.results[0]["out_0"]
```
